# Optimizing a Trainium2 kernel written in Bass

```python
import math
import jax, jax.numpy as jnp
from jax import lax
import numpy as np

D_MODEL = 1024
BATCH = 1
SEQ = 512
DEPTH = 2

MIX_WIDTH = D_MODEL
SSM_WIDTH = MIX_WIDTH // 2
POOL_WIDTH = MIX_WIDTH - SSM_WIDTH
SSM_GROUP = 16
SSM_GROUPS = SSM_WIDTH // SSM_GROUP
SSM_STATE = 64
POOL_WINDOWS = (2, 4, 8, 16)
POOL_GROUPS = 4
POOL_GROUP_WIDTH = POOL_WIDTH // POOL_GROUPS
PEER_HEADS = 8
PEER_N_KEYS = 128
PEER_N_EXPERTS = PEER_N_KEYS * PEER_N_KEYS
PEER_KEY_DIM = 256
PEER_HALF = PEER_KEY_DIM // 2
PEER_TOPK = 16
PEER_CHUNK = 128
RMS_EPS = 1e-6
DT_MIN = 1e-3
DT_MAX = 1e-1

kernel_name = 'hybrid_s5_pool_peer'

def rmsnorm(x, g):
    xf = x.astype(jnp.float32)
    y = xf * lax.rsqrt(jnp.mean(xf * xf, axis=-1, keepdims=True) + RMS_EPS)
    return (y * g.astype(jnp.float32)).astype(x.dtype)

def _complex_affine_combine(left, right):
    a1r, a1i, b1r, b1i = left
    a2r, a2i, b2r, b2i = right
    ar = a1r * a2r - a1i * a2i
    ai = a1r * a2i + a1i * a2r
    br = a2r * b1r - a2i * b1i + b2r
    bi = a2r * b1i + a2i * b1r + b2i
    return ar, ai, br, bi

def s5_mixer(u, a_re, a_im, log_dt, b_re, b_im, c_re, c_im, d_skip, w_glu, b_glu):
    bsz, seq, _ = u.shape
    f32 = jnp.float32
    uf = u.astype(f32).reshape(bsz, seq, SSM_GROUPS, SSM_GROUP)
    lam_re = a_re.astype(f32)
    lam_im = a_im.astype(f32)
    dt = jnp.exp(log_dt.astype(f32))[:, None]
    decay = jnp.exp(lam_re * dt)
    abar_re = decay * jnp.cos(lam_im * dt)
    abar_im = decay * jnp.sin(lam_im * dt)
    inv_den = 1.0 / (lam_re * lam_re + lam_im * lam_im)
    num_re = abar_re - 1.0
    zoh_re = (num_re * lam_re + abar_im * lam_im) * inv_den
    zoh_im = (abar_im * lam_re - num_re * lam_im) * inv_den
    bu_re = jnp.einsum('blgh,gph->blgp', uf, b_re.astype(f32))
    bu_im = jnp.einsum('blgh,gph->blgp', uf, b_im.astype(f32))
    in_re = zoh_re * bu_re - zoh_im * bu_im
    in_im = zoh_re * bu_im + zoh_im * bu_re
    a_seq_re = jnp.broadcast_to(abar_re, in_re.shape)
    a_seq_im = jnp.broadcast_to(abar_im, in_re.shape)
    _, _, s_re, s_im = lax.associative_scan(
        _complex_affine_combine, (a_seq_re, a_seq_im, in_re, in_im), axis=1)
    y = (jnp.einsum('blgp,ghp->blgh', s_re, c_re.astype(f32))
         - jnp.einsum('blgp,ghp->blgh', s_im, c_im.astype(f32))
         + d_skip.astype(f32) * uf)
    y = jax.nn.gelu(y.reshape(bsz, seq, SSM_WIDTH), approximate=False)
    y = y * jax.nn.sigmoid(y @ w_glu.astype(f32) + b_glu.astype(f32))
    return y.astype(u.dtype)

def pool_mixer(u, w_pool, pool_scale):
    bsz, seq, _ = u.shape
    f32 = jnp.float32
    uf = u.astype(f32).reshape(bsz, seq, POOL_GROUPS, POOL_GROUP_WIDTH)
    cs = jnp.cumsum(uf, axis=1)
    pos = jnp.arange(1, seq + 1, dtype=f32)
    outs = []
    for gi, win in enumerate(POOL_WINDOWS):
        csg = cs[:, :, gi]
        lagged = jnp.pad(csg, ((0, 0), (win, 0), (0, 0)))[:, :seq]
        count = jnp.minimum(pos, float(win))[:, None]
        outs.append((csg - lagged) / count - uf[:, :, gi])
    pooled = jnp.stack(outs, axis=2)
    mixed = jnp.einsum('blgc,gcd->blgd', pooled, w_pool.astype(f32))
    y = mixed.reshape(bsz, seq, POOL_WIDTH) * pool_scale.astype(f32)
    return y.astype(u.dtype)

def peer_ffn(h, w_q, k1, k2, u_tab, v_tab):
    bsz, seq, dm = h.shape
    q = jnp.einsum('bld,dk->blk', h, w_q).reshape(bsz, seq, PEER_HEADS, 2, PEER_HALF)
    s1 = jnp.einsum('blhk,nk->blhn', q[..., 0, :], k1).astype(jnp.float32)
    s2 = jnp.einsum('blhk,nk->blhn', q[..., 1, :], k2).astype(jnp.float32)
    v1, i1 = lax.top_k(s1, PEER_TOPK)
    v2, i2 = lax.top_k(s2, PEER_TOPK)
    cand_score = (v1[..., :, None] + v2[..., None, :]).reshape(bsz, seq, PEER_HEADS, PEER_TOPK * PEER_TOPK)
    cand_idx = (i1[..., :, None] * PEER_N_KEYS + i2[..., None, :]).reshape(bsz, seq, PEER_HEADS, PEER_TOPK * PEER_TOPK)
    best, sel = lax.top_k(cand_score, PEER_TOPK)
    experts = jnp.take_along_axis(cand_idx, sel, axis=-1)
    gates = jax.nn.softmax(best, axis=-1).astype(h.dtype)
    n_chunks = (bsz * seq) // PEER_CHUNK
    hc = h.reshape(n_chunks, PEER_CHUNK, dm)
    ec = experts.reshape(n_chunks, PEER_CHUNK, PEER_HEADS, PEER_TOPK)
    gc = gates.reshape(n_chunks, PEER_CHUNK, PEER_HEADS, PEER_TOPK)

    def chunk(args):
        xc, ei, gi = args
        u_sel = jnp.take(u_tab, ei, axis=0)
        act = jax.nn.gelu(jnp.einsum('cd,chkd->chk', xc, u_sel), approximate=False) * gi
        v_sel = jnp.take(v_tab, ei, axis=0)
        return jnp.einsum('chk,chkd->cd', act, v_sel)

    out = lax.map(chunk, (hc, ec, gc))
    return out.reshape(bsz, seq, dm)

def setup_inputs(seed: int = 0) -> dict:
    key = jax.random.key(seed)
    ks = jax.random.split(key, 26)
    f32 = jnp.float32

    def nrm(k, shape, scale):
        return jax.random.normal(k, shape, f32) * scale

    def gain(k, shape):
        return 1.0 + 0.05 * jax.random.normal(k, shape, f32)

    nl, g, p, hh = DEPTH, SSM_GROUPS, SSM_STATE, SSM_GROUP
    x = jax.random.normal(ks[0], (BATCH, SEQ, D_MODEL), f32)
    norm_mix = gain(ks[1], (nl, D_MODEL))
    w_in = nrm(ks[2], (nl, D_MODEL, MIX_WIDTH), D_MODEL ** -0.5)
    a_re = -0.5 + 0.01 * jax.random.normal(ks[3], (nl, g, p), f32)
    a_im = math.pi * jnp.arange(p, dtype=f32) + 0.01 * jax.random.normal(ks[4], (nl, g, p), f32)
    log_dt = jax.random.uniform(ks[5], (nl, g), f32, math.log(DT_MIN), math.log(DT_MAX))
    b_re = nrm(ks[6], (nl, g, p, hh), (2 * hh) ** -0.5)
    b_im = nrm(ks[7], (nl, g, p, hh), (2 * hh) ** -0.5)
    c_re = nrm(ks[8], (nl, g, hh, p), (2 * p) ** -0.5)
    c_im = nrm(ks[9], (nl, g, hh, p), (2 * p) ** -0.5)
    d_skip = nrm(ks[10], (nl, g, hh), 1.0)
    w_glu = nrm(ks[11], (nl, SSM_WIDTH, SSM_WIDTH), SSM_WIDTH ** -0.5)
    b_glu = nrm(ks[12], (nl, SSM_WIDTH), 0.02)
    w_pool = nrm(ks[13], (nl, POOL_GROUPS, POOL_GROUP_WIDTH, POOL_GROUP_WIDTH), POOL_GROUP_WIDTH ** -0.5)
    pool_scale = gain(ks[14], (nl, POOL_WIDTH))
    g_out_ssm = gain(ks[15], (nl, SSM_WIDTH))
    g_out_pool = gain(ks[16], (nl, POOL_WIDTH))
    w_out = nrm(ks[17], (nl, MIX_WIDTH, D_MODEL), MIX_WIDTH ** -0.5)
    norm_ffn = gain(ks[18], (nl, D_MODEL))
    w_q = nrm(ks[19], (nl, D_MODEL, PEER_HEADS * PEER_KEY_DIM), D_MODEL ** -0.5)
    k1 = nrm(ks[20], (nl, PEER_N_KEYS, PEER_HALF), PEER_HALF ** -0.5)
    k2 = nrm(ks[21], (nl, PEER_N_KEYS, PEER_HALF), PEER_HALF ** -0.5)
    u_experts = nrm(ks[22], (nl, PEER_N_EXPERTS, D_MODEL), D_MODEL ** -0.5)
    v_experts = nrm(ks[23], (nl, PEER_N_EXPERTS, D_MODEL), PEER_HEADS ** -0.5)
    norm_final = gain(ks[24], (D_MODEL,))
    return {'x': x, 'norm_mix': norm_mix, 'w_in': w_in, 'a_re': a_re, 'a_im': a_im,
            'log_dt': log_dt, 'b_re': b_re, 'b_im': b_im, 'c_re': c_re, 'c_im': c_im,
            'd_skip': d_skip, 'w_glu': w_glu, 'b_glu': b_glu, 'w_pool': w_pool,
            'pool_scale': pool_scale, 'g_out_ssm': g_out_ssm, 'g_out_pool': g_out_pool,
            'w_out': w_out, 'norm_ffn': norm_ffn, 'w_q': w_q, 'k1': k1, 'k2': k2,
            'u_experts': u_experts, 'v_experts': v_experts, 'norm_final': norm_final}

def reference(x, norm_mix, w_in, a_re, a_im, log_dt, b_re, b_im, c_re, c_im, d_skip,
              w_glu, b_glu, w_pool, pool_scale, g_out_ssm, g_out_pool, w_out, norm_ffn,
              w_q, k1, k2, u_experts, v_experts, norm_final):
    for i in range(DEPTH):
        hn = rmsnorm(x, norm_mix[i])
        proj = jnp.einsum('bld,dm->blm', hn, w_in[i])
        u_ssm = proj[..., :SSM_WIDTH]
        u_pool = proj[..., SSM_WIDTH:]
        y_ssm = s5_mixer(u_ssm, a_re[i], a_im[i], log_dt[i], b_re[i], b_im[i],
                         c_re[i], c_im[i], d_skip[i], w_glu[i], b_glu[i])
        y_pool = pool_mixer(u_pool, w_pool[i], pool_scale[i])
        mixed = jnp.concatenate([rmsnorm(y_ssm, g_out_ssm[i]), rmsnorm(y_pool, g_out_pool[i])], axis=-1)
        x = x + jnp.einsum('blm,md->bld', mixed, w_out[i])
        x = x + peer_ffn(rmsnorm(x, norm_ffn[i]), w_q[i], k1[i], k2[i], u_experts[i], v_experts[i])
    return rmsnorm(x, norm_final)


_drawn_inputs = setup_inputs


def setup_inputs(seed=0):
    import zlib

    import numpy as np

    out = dict(_drawn_inputs(seed))
    spreads = {}
    factors = {'a_re': 8.0, 'b_glu': 3.921}
    for name, (base, spread) in spreads.items():
        noise = np.random.default_rng([zlib.crc32(name.encode()), seed]).standard_normal(out[name].shape)
        drawn = base * np.exp(spread * noise) if base else spread * noise
        out[name] = __import__('jax').numpy.asarray(drawn.astype(out[name].dtype))
    for name, factor in factors.items():
        out[name] = (out[name] * factor).astype(out[name].dtype)
    return out
```

```python
import math
from contextlib import ExitStack

import concourse.bass as bass
from concourse import mybir

F32 = mybir.dt.float32
I32 = mybir.dt.int32
U32 = mybir.dt.uint32
ALU = mybir.AluOpType
ACT = mybir.ActivationFunctionType
AX_X = mybir.AxisListType.X

P = 128
D = 1024
SEQ = 512
DEPTH = 2
TILES = SEQ // P
STEPS = DEPTH * TILES
KD = D // P
SSM = D // 2
CT = SSM // P
GROUP_CH = 16
STATE = 64
BLOCKS = (SSM // GROUP_CH) * STATE // P
BLOCK_CH = 2 * GROUP_CH
HALF = P // 2
WINDOWS = (2, 4, 8, 16)
HALO = 16
HEADS = 8
KEYS = 128
TOPK = 16
CHOICES = HEADS * TOPK
EXPERTS = KEYS * KEYS
EPS = 1e-6
PAIRS = HEADS // 2
PAIR = 2 * TOPK
SLOTS = 6
WIN_SLOTS = 3
DIAGS = 4
DOTS = 8
LOWEST = -3.0e38
ROUND = 12582912.0
TWO_PI_1 = 6.28125
TWO_PI_2 = 0.0019350051879882812
TWO_PI_3 = 2 * math.pi - TWO_PI_1 - TWO_PI_2
PI_BELOW = 3.1415925

QT, REST, CAND, LEFT, HOT, MISC = 1024, 1536, 1792, 2048, 2304, 2816

LAM_RE, LAM_IM, LOG_DT = 0, BLOCKS, 2 * BLOCKS
G_MIX = 3 * BLOCKS
D_SKIP = G_MIX + KD
B_GLU = D_SKIP + CT
P_SCALE = B_GLU + CT
G_SSM = P_SCALE + CT
G_POOL = G_SSM + CT
PARAMS = G_POOL + CT
BC = BLOCKS * GROUP_CH


def slot_plan():
    short = (-CHOICES % SLOTS) // 2
    while (CHOICES - short * (SLOTS - 2)) % SLOTS:
        short += 1
    full = (CHOICES - short * (SLOTS - 2)) // SLOTS
    rounds = [SLOTS] * (full - full // 4) + [SLOTS - 2] * short + [SLOTS] * (full // 4)
    slot_of = [j for n in rounds for j in range(n)]
    last = {j: j - SLOTS for j in range(SLOTS)}
    taken, takes, turn, turns = 0, [], [], {j: 0 for j in range(SLOTS)}
    for k, j in enumerate(slot_of):
        need = last[j] + 1 + SLOTS
        takes.append(max(0, need - taken))
        taken = max(taken, need)
        last[j] = k
        turn.append(turns[j])
        turns[j] += 1
    takes.append(CHOICES - taken)
    return slot_of, turn, turns, takes


SLOT_OF, TURN, TURNS, FREED = slot_plan()


def build(nc, x, win, wout, wglu, wpool, wq, keys, params, bc, gffn, gfinal, uv, x_state, out):
    ctx = ExitStack()
    with ctx:
        def sb(name, shape, dt=F32):
            return ctx.enter_context(nc.sbuf_tensor(name, shape, dt))

        def sem(name):
            return ctx.enter_context(nc.semaphore(name))

        wq_sb = sb("wq_sb", [P, KD, 2 * HEADS * KEYS])
        wout_sb = sb("wout_sb", [P, KD, D])
        wglu_sb = sb("wglu_sb", [P, CT, SSM])
        wpool_sb = sb("wpool_sb", [P, CT, P])
        keys_sb = sb("keys_sb", [P, 2, KEYS])
        par = sb("par", [P, PARAMS])
        gffn_sb = sb("gffn_sb", [P, D])
        slots = [sb(f"slot{j}", [P, 2 * D]) for j in range(SLOTS)]
        h_dot = sb("h_dot", [P, D])
        rows_of = sb("rows_of", [P, CHOICES], I32)
        gates = sb("gates", [P, CHOICES])
        dots = sb("dots", [P, DOTS])
        gelu_sb = sb("gelu_sb", [P, DOTS])
        diag = sb("diag", [P, DIAGS, P])
        x_pend = sb("x_pend", [P, D])
        x_front = sb("x_front", [P, D])
        h_next = sb("h_next", [P, D])
        hT = sb("hT", [P, KD, P])
        uT = sb("uT", [P, CT, P])
        poolT = sb("poolT", [P, CT, HALO + P])
        work = sb("work", [P, 3 * D])
        tab_c = sb("tab_c", [P, BLOCKS, HALF])
        tab_s = sb("tab_s", [P, BLOCKS, HALF])
        bT = [sb("bT_re", [P, CT, P]), sb("bT_im", [P, CT, P])]
        cw = [sb("cw_re", [P, BLOCKS, BLOCK_CH]), sb("cw_im", [P, BLOCKS, BLOCK_CH])]
        state = sb("state", [P, 2, BLOCKS])
        small = sb("small", [P, 12, BLOCKS])
        hand = sb("hand", [P, 6, 4])
        stat = sb("stat", [P, 24])
        v16 = sb("v16", [P, 2, TOPK])
        best = sb("best", [P, HEADS, TOPK])
        sel = sb("sel", [P, HEADS, TOPK], U32)
        i12 = sb("i12", [P, HEADS, 2, TOPK], U32)
        hsum = sb("hsum", [P, 2])
        ident = sb("ident", [P, P])
        ones = sb("ones", [P, 1])
        mhalf = sb("mhalf", [P, TILES - 1])
        iota16 = sb("iota16", [P, TOPK])
        invcnt = sb("invcnt", [P, CT, HALO])

        acc = ctx.enter_context(nc.psum_tensor("acc", [P, D], F32))
        bank = ctx.enter_context(nc.psum_tensor("bank", [P, 4, 512], F32))
        ff = ctx.enter_context(nc.psum_tensor("ff", [P, 2, 512], F32))

        win_sb = [work[:, i * D:(i + 1) * D].rearrange("p (k n) -> p k n", k=KD) for i in range(WIN_SLOTS)]

        def piece(a, *shape):
            n = math.prod(shape)
            v = work[:, a:a + n]
            if len(shape) == 2:
                return v.rearrange("p (a b) -> p a b", a=shape[0])
            if len(shape) == 3:
                return v.rearrange("p (a b c) -> p a b c", a=shape[0], b=shape[1])
            return v

        final_in = sem("final_in")
        par_in = sem("par_in")
        bc_in = sem("bc_in")
        weights_in = sem("weights_in")
        wout_in = sem("wout_in")
        wq_in = sem("wq_in")
        x_in = sem("x_in")
        win_in = [sem(f"win_in{i}") for i in range(WIN_SLOTS)]
        row_in = [sem(f"row_in{j}") for j in range(SLOTS)]
        x_stored = sem("x_stored")
        out_stored = sem("out_stored")
        dve_own = sem("dve_own")
        act_own = sem("act_own")
        pool_own = sem("pool_own")
        consts_pe = sem("consts_pe")
        consts_act = sem("consts_act")
        consts_dve = sem("consts_dve")
        slot_free_pool = sem("slot_free_pool")
        idx_pool = sem("idx_pool")
        dot_act = sem("dot_act")
        gates_act = sem("gates_act")
        diag_pe = sem("diag_pe")
        diag_free_act = sem("diag_free_act")
        acc_dve = sem("acc_dve")
        mix_done_sp = sem("mix_done_sp")
        final_sp = sem("final_sp")
        acc_free_pe = sem("acc_free_pe")
        out_sp = sem("out_sp")
        sq_dve = sem("sq_dve")
        ms_pool = sem("ms_pool")
        rstd_dve = sem("rstd_dve")
        xn_pe = sem("xn_pe")
        hTp_dve = sem("hTp_dve")
        hT_pe = sem("hT_pe")
        win_used_sp = sem("win_used_sp")
        projA_act = sem("projA_act")
        projB_act = sem("projB_act")
        halo_act = sem("halo_act")
        uT_pe = sem("uT_pe")
        uT_dve = sem("uT_dve")
        poolT_dve = sem("poolT_dve")
        poolT_pe = sem("poolT_pe")
        bu_dve = sem("bu_dve")
        bu_free_pe = sem("bu_free_pe")
        s_pe = sem("s_pe")
        s_used_dve = sem("s_used_dve")
        sums_dve = sem("sums_dve")
        y_dve = sem("y_dve")
        y_act = sem("y_act")
        y1_pe = sem("y1_pe")
        glu_act = sem("glu_act")
        sg_dve = sem("sg_dve")
        mixA_pe = sem("mixA_pe")
        pooled_pe = sem("pooled_pe")
        poolmix_dve = sem("poolmix_dve")
        mixB_pe = sem("mixB_pe")
        outA_dve = sem("outA_dve")
        xmid_act = sem("xmid_act")
        h_pe = sem("h_pe")
        hT2_act = sem("hT2_act")
        hT2_pe = sem("hT2_pe")
        q_act = sem("q_act")
        qT_pe = sem("qT_pe")
        score_dve = sem("score_dve")
        score_free_pe = sem("score_free_pe")
        e_act = sem("e_act")
        e_dve = sem("e_dve")
        front_done_sp = sem("front_done_sp")
        xfront_free_sp = sem("xfront_free_sp")
        xpend_free_dve = sem("xpend_free_dve")
        set_act = sem("set_act")
        set_dve = sem("set_dve")
        bd_pe = sem("bd_pe")
        bdT_dve = sem("bdT_dve")

        block = ctx.enter_context(nc.Block())
        final = [wq_sb[:, i, 0:D] for i in range(5)]

        @block.sync
        def _(sp):
            def load_win(m, layer):
                sp.dma_start(win_sb[m % WIN_SLOTS], win[layer, m]).then_inc(win_in[m % WIN_SLOTS], 16)

            def loads(f, layer, first, begin=False):
                if not begin:
                    sp.wait_ge(mix_done_sp, 1)
                    sp.sem_inc(mix_done_sp, -1)
                load_win(0, layer)
                if not begin:
                    sp.wait_ge(xfront_free_sp, 1)
                    sp.sem_inc(xfront_free_sp, -1)
                src = x_state if layer else x
                row = (f - layer * TILES) * P
                sp.dma_start(x_front[:, :], src[bass.ds(row, P), :]).then_inc(x_in, 16)
                if not begin:
                    sp.wait_ge(front_done_sp, 1)
                    sp.sem_inc(front_done_sp, -1)
                if first:
                    sp.dma_start(par[:, :], params[layer]).then_inc(par_in, 16)
                    sp.dma_start(hT[:, :, :].rearrange("p a b -> p (a b)"), bc[layer]).then_inc(bc_in, 16)
                for m in range(1, WIN_SLOTS):
                    load_win(m, layer)
                if first:
                    sp.dma_start(wglu_sb[:, :, :], wglu[layer]).then_inc(weights_in, 16)
                    sp.dma_start(wpool_sb[:, :, :], wpool[layer]).then_inc(weights_in, 16)
                    sp.dma_start(keys_sb[:, :, :], keys[layer]).then_inc(weights_in, 16)
                    sp.dma_start(gffn_sb[:, :], gffn[layer]).then_inc(weights_in, 16)
                for m in range(WIN_SLOTS, KD):
                    sp.wait_ge(win_used_sp, 1)
                    sp.sem_inc(win_used_sp, -1)
                    load_win(m, layer)
                if first:
                    sp.dma_start(wout_sb[:, :, :], wout[layer]).then_inc(wout_in, 16)
                    sp.dma_start(wq_sb[:, :, :], wq[layer]).then_inc(wq_in, 16)

            def store(s, layer):
                sp.wait_ge(out_sp, 1)
                sp.sem_inc(out_sp, -1)
                row = (s - layer * TILES) * P
                sp.dma_start(x_state[bass.ds(row, P), :], x_pend[:, :]).then_inc(x_stored, 16)
                sp.wait_ge(x_stored, (s + 1) * 16)
                sp.sem_inc(xpend_free_dve, 1)

            sp.sem_inc(xpend_free_dve, 1)
            loads(0, 0, True, begin=True)
            for layer in range(DEPTH):
                s0 = layer * TILES
                with sp.Fori(s0, s0 + TILES - 1) as s:
                    loads(s + 1, layer, False)
                    store(s, layer)
                if layer + 1 < DEPTH:
                    loads(s0 + TILES, layer + 1, True)
                    store(s0 + TILES - 1, layer)
            sp.wait_ge(mix_done_sp, 1)
            sp.sem_inc(mix_done_sp, -1)
            sp.wait_ge(xfront_free_sp, 1)
            sp.sem_inc(xfront_free_sp, -1)
            sp.wait_ge(front_done_sp, 1)
            sp.sem_inc(front_done_sp, -1)
            sp.dma_start(final[0], gfinal).then_inc(final_in, 16)
            for t in range(TILES - 1):
                sp.dma_start(final[1 + t], x_state[t * P:(t + 1) * P, :]).then_inc(final_in, 16)
            sp.wait_ge(final_sp, 1)
            sp.sem_inc(final_sp, -1)
            for t in range(TILES - 1):
                sp.dma_start(out[t * P:(t + 1) * P, :], final[1 + t]).then_inc(out_stored, 16)
            sp.wait_ge(out_sp, 1)
            sp.sem_inc(out_sp, -1)
            sp.dma_start(out[(TILES - 1) * P:TILES * P, :], x_pend[:, :]).then_inc(out_stored, 16)
            sp.wait_ge(out_stored, 16 * TILES)

        @block.gpsimd
        def _(pool):
            def power(a, n):
                pool.wait_ge(ms_pool, 1)
                pool.sem_inc(ms_pool, -1)
                nc.gpsimd.tensor_tensor(stat[:, a + n:a + 2 * n], stat[:, a:a + n], mhalf[:, 0:n],
                                        ALU.pow).then_inc(rstd_dve, 1)

            def choices(a, b):
                for k in range(a, b):
                    if k % PAIR == 0:
                        pool.wait_ge(idx_pool, 1)
                        pool.sem_inc(idx_pool, -1)
                    if FREED[k]:
                        pool.wait_ge(slot_free_pool, FREED[k])
                        pool.sem_inc(slot_free_pool, -FREED[k])
                    nc.gpsimd.indirect_dma_start(
                        out=slots[SLOT_OF[k]][:, :], out_offset=None, in_=uv[:, :],
                        in_offset=bass.IndirectOffsetOnAxis(ap=rows_of[:, k:k + 1], axis=0),
                    ).then_inc(row_in[SLOT_OF[k]], 16)

            def step(more):
                if more:
                    choices(0, 14)
                    power(0, 1)
                    choices(14, 95)
                    power(4, 2)
                    choices(95, 103)
                    power(8, 1)
                    choices(103, CHOICES)
                else:
                    choices(0, 64)
                    power(12, TILES - 1)
                    choices(64, CHOICES)

            nc.gpsimd.memset(ident[:, :], 0.0).then_inc(pool_own, 1)
            pool.wait_ge(pool_own, 1)
            pool.sem_inc(pool_own, -1)
            nc.gpsimd.affine_select(out=ident[:, :], in_=ident[:, :], compare_op=ALU.not_equal, fill=1.0,
                                    base=0, pattern=[[-1, P]], channel_multiplier=1)
            nc.gpsimd.memset(ones[:, :], 1.0)
            nc.gpsimd.memset(mhalf[:, :], -0.5)
            nc.gpsimd.iota(iota16[:, :], pattern=[[1, TOPK]], base=0, channel_multiplier=0,
                           allow_small_or_imprecise_dtypes=True).then_inc(pool_own, 1)
            pool.wait_ge(pool_own, 1)
            pool.sem_inc(pool_own, -1)
            pool.sem_inc(consts_pe, 1)
            pool.sem_inc(consts_act, 1)
            pool.sem_inc(consts_dve, 1)
            pool.sem_inc(slot_free_pool, SLOTS)
            power(0, 1)
            power(4, 2)
            power(8, 1)
            for layer in range(DEPTH):
                s0 = layer * TILES
                with pool.Fori(s0, s0 + TILES - 1):
                    step(True)
                if layer + 1 < DEPTH:
                    step(True)
            step(False)
            power(18, 1)

        @block.scalar
        def _(act):
            def choices(a, b):
                for k in range(a, b):
                    d = k % DOTS
                    if k % PAIR == 0:
                        act.wait_ge(gates_act, 1)
                        act.sem_inc(gates_act, -1)
                    act.wait_ge(dot_act, 1)
                    act.sem_inc(dot_act, -1)
                    nc.scalar.activation(gelu_sb[:, d:d + 1], dots[:, d:d + 1], ACT.Gelu).then_inc(act_own, 1)
                    act.wait_ge(act_own, 1)
                    act.sem_inc(act_own, -1)
                    nc.scalar.activation(dots[:, d:d + 1], gelu_sb[:, d:d + 1], ACT.Copy, scale=gates[:, k:k + 1]).then_inc(act_own, 1)
                    act.wait_ge(act_own, 1)
                    act.sem_inc(act_own, -1)
                    act.wait_ge(diag_free_act, 1)
                    act.sem_inc(diag_free_act, -1)
                    nc.scalar.activation(diag[:, k % DIAGS, :], ident[:, :], ACT.Copy, scale=dots[:, d:d + 1]).then_inc(diag_pe, 1)

            def setup(layer):
                act.wait_ge(par_in, 16 * (layer + 1))
                nc.scalar.activation(small[:, 0, :], par[:, LOG_DT:LOG_DT + BLOCKS], ACT.Exp).then_inc(set_dve, 1)
                act.wait_ge(set_act, 1)
                act.sem_inc(set_act, -1)
                nc.scalar.activation(small[:, 3, :], small[:, 1, :], ACT.Exp).then_inc(act_own, 1)
                act.wait_ge(act_own, 1)
                act.sem_inc(act_own, -1)
                nc.scalar.activation(small[:, 4, :], small[:, 2, :], ACT.Sin, scale=0.5)
                nc.scalar.activation(small[:, 5, :], small[:, 2, :], ACT.Sin).then_inc(set_dve, 1)

            def square_x(f):
                act.wait_ge(x_in, 16 * (f + 1))
                nc.scalar.activation(h_next[:, :], x_front[:, :], ACT.Square, accum_out=stat[:, 2:3]).then_inc(sq_dve, 1)

            def ssm_input():
                act.wait_ge(projA_act, 1)
                act.sem_inc(projA_act, -1)
                nc.scalar.activation(uT[:, :, :], bank[:, 2, :].rearrange("p (a b) -> p a b", a=CT), ACT.Copy).then_inc(act_own, 1)
                act.wait_ge(act_own, 1)
                act.sem_inc(act_own, -1)
                act.sem_inc(uT_pe, 1)
                act.sem_inc(uT_dve, 1)

            def pool_input():
                act.wait_ge(projB_act, 1)
                act.sem_inc(projB_act, -1)
                act.wait_ge(halo_act, 1)
                act.sem_inc(halo_act, -1)
                nc.scalar.activation(poolT[:, :, HALO:], bank[:, 3, :].rearrange("p (a b) -> p a b", a=CT), ACT.Copy).then_inc(act_own, 1)
                act.wait_ge(act_own, 1)
                act.sem_inc(act_own, -1)
                act.sem_inc(poolT_dve, 1)
                act.sem_inc(poolT_pe, 1)

            def gelu_y():
                act.wait_ge(y_act, 1)
                act.sem_inc(y_act, -1)
                nc.scalar.activation(uT[:, :, :], uT[:, :, :], ACT.Gelu).then_inc(y1_pe, 1)

            def glu_gate():
                act.wait_ge(glu_act, 1)
                act.sem_inc(glu_act, -1)
                for n in range(CT):
                    last = nc.scalar.activation(piece(n * P, P), ff[:, 1, n * P:(n + 1) * P], ACT.Sigmoid,
                                                bias=par[:, B_GLU + n:B_GLU + n + 1])
                last.then_inc(sg_dve, 1)

            def square_mixed():
                act.wait_ge(xmid_act, 1)
                act.sem_inc(xmid_act, -1)
                nc.scalar.activation(h_next[:, :], x_front[:, :], ACT.Square, accum_out=stat[:, 10:11]).then_inc(sq_dve, 1)

            def h_turned():
                act.wait_ge(hT2_act, 1)
                act.sem_inc(hT2_act, -1)
                nc.scalar.activation(hT[:, :, :].rearrange("p a b -> p (a b)"),
                                     bank[:, 0:2, :].rearrange("p a b -> p (a b)"), ACT.Copy).then_inc(hT2_pe, 1)

            def query(h):
                act.wait_ge(q_act, 1)
                act.sem_inc(q_act, -1)
                nc.scalar.activation(piece(QT + 256 * (h % 2), 256), bank[:, 2 + h % 2, 0:256], ACT.Copy).then_inc(qT_pe, 1)

            def exp_scores(n):
                act.wait_ge(e_act, 1)
                act.sem_inc(e_act, -1)
                nc.scalar.activation(gates[:, n * PAIR:(n + 1) * PAIR], gates[:, n * PAIR:(n + 1) * PAIR], ACT.Exp).then_inc(e_dve, 1)

            def step(f, layer_f, first, more):
                choices(0, 3)
                query(2)
                choices(3, 7)
                query(3)
                if more:
                    choices(7, 8)
                    square_x(f)
                    choices(8, 10)
                else:
                    choices(7, 10)
                query(4)
                choices(10, 14)
                query(5)
                choices(14, 15)
                exp_scores(1)
                choices(15, 17)
                query(6)
                choices(17, 21)
                query(7)
                choices(21, 22)
                exp_scores(2)
                choices(22, 29)
                exp_scores(3)
                if more:
                    choices(29, 31)
                    if first:
                        setup(layer_f)
                    choices(31, 36)
                    ssm_input()
                    choices(36, 42)
                    pool_input()
                    choices(42, 80)
                    gelu_y()
                    choices(80, 86)
                    glu_gate()
                    choices(86, 99)
                    square_mixed()
                    choices(99, 106)
                    h_turned()
                    choices(106, 110)
                    query(0)
                    choices(110, 113)
                    query(1)
                    choices(113, 120)
                    exp_scores(0)
                    choices(120, CHOICES)
                else:
                    choices(29, CHOICES)

            act.wait_ge(consts_act, 1)
            act.sem_inc(consts_act, -1)
            act.sem_inc(diag_free_act, DIAGS - 1)
            square_x(0)
            setup(0)
            ssm_input()
            pool_input()
            gelu_y()
            glu_gate()
            square_mixed()
            h_turned()
            query(0)
            query(1)
            exp_scores(0)
            for layer in range(DEPTH):
                s0 = layer * TILES
                with act.Fori(s0, s0 + TILES - 1) as s:
                    step(s + 1, layer, False, True)
                if layer + 1 < DEPTH:
                    step(s0 + TILES, layer + 1, True, True)
            step(None, None, False, False)

        @block.tensor
        def _(pe):
            def choices(a, b):
                for k in range(a, b):
                    if k == 0:
                        pe.wait_ge(acc_free_pe, 1)
                        pe.sem_inc(acc_free_pe, -1)
                    pe.wait_ge(diag_pe, 1)
                    pe.sem_inc(diag_pe, -1)
                    nc.tensor.matmul(acc[:, 0:512], diag[:, k % DIAGS, :], slots[SLOT_OF[k]][:, D:D + 512],
                                     start=k == 0, stop=k == CHOICES - 1, skip_group_check=True).then_inc(diag_free_act, 1)
                    nc.tensor.matmul(acc[:, 512:1024], diag[:, k % DIAGS, :], slots[SLOT_OF[k]][:, D + 512:2 * D],
                                     start=k == 0, stop=k == CHOICES - 1, skip_group_check=True).then_inc(slot_free_pool, 1)
                if b == CHOICES:
                    pe.drain().then_inc(acc_dve, 1)

            def turn_maps():
                pe.wait_ge(bd_pe, 1)
                pe.sem_inc(bd_pe, -1)
                for ri in range(2):
                    for q in range(CT):
                        last = nc.tensor.transpose(bank[:, ri, q * P:(q + 1) * P],
                                                   h_next[:, ri * 512 + q * P:ri * 512 + (q + 1) * P], ident[:, :])
                last.then_inc(bdT_dve, 1)

            def turn_x():
                pe.wait_ge(xn_pe, 1)
                pe.sem_inc(xn_pe, -1)
                for k in range(KD):
                    last = nc.tensor.transpose(bank[:, k // 4, (k % 4) * P:(k % 4 + 1) * P],
                                               h_next[:, k * P:(k + 1) * P], ident[:, :])
                last.then_inc(hTp_dve, 1)

            def project(f, m):
                if m == 0:
                    pe.wait_ge(hT_pe, 1)
                    pe.sem_inc(hT_pe, -1)
                turns = (KD - m % WIN_SLOTS + WIN_SLOTS - 1) // WIN_SLOTS
                pe.wait_ge(win_in[m % WIN_SLOTS], (f * turns + m // WIN_SLOTS + 1) * 16)
                for k in range(KD):
                    last = nc.tensor.matmul(bank[:, 2 + m // CT, (m % CT) * P:(m % CT + 1) * P],
                                            win_sb[m % WIN_SLOTS][:, k, :], hT[:, k, :], start=k == 0, stop=k == KD - 1)
                    if k == 0 and 1 <= m <= KD - WIN_SLOTS:
                        last.then_inc(win_used_sp, 1)
                if m == CT - 1:
                    last.then_inc(projA_act, 1)
                if m == KD - 1:
                    last.then_inc(projB_act, 1)

            def state_inputs(q):
                if q == 0:
                    pe.wait_ge(uT_pe, 1)
                    pe.sem_inc(uT_pe, -1)
                    pe.wait_ge(poolT_pe, 1)
                    pe.sem_inc(poolT_pe, -1)
                else:
                    pe.wait_ge(bu_free_pe, 1)
                    pe.sem_inc(bu_free_pe, -1)
                for i in range(4):
                    for ri in range(2):
                        last = nc.tensor.matmul(bank[:, i, ri * P:(ri + 1) * P], bT[ri][32 * i:32 * i + 32, q, :],
                                                uT[32 * i:32 * i + 32, q, :], start=True, stop=True)
                last.then_inc(bu_dve, 1)

            def state_outputs(q):
                pe.wait_ge(s_pe, 1)
                pe.sem_inc(s_pe, -1)
                a = (q % 2) * D
                for i in range(4):
                    for ri in range(2):
                        last = nc.tensor.matmul(ff[32 * i:32 * i + 32, 0, q * P:(q + 1) * P], cw[ri][:, 4 * q + i, :],
                                                work[:, a + ri * 512 + i * P:a + ri * 512 + (i + 1) * P],
                                                start=ri == 0, stop=ri == 1)
                if q == 3:
                    last.then_inc(y_dve, 1)
                else:
                    last.then_inc(s_used_dve, 1)

            def glu(n):
                if n == 0:
                    pe.wait_ge(y1_pe, 1)
                    pe.sem_inc(y1_pe, -1)
                for k in range(CT):
                    last = nc.tensor.matmul(ff[:, 1, n * P:(n + 1) * P], wglu_sb[:, k, n * P:(n + 1) * P], uT[:, k, :],
                                            start=k == 0, stop=k == CT - 1)
                if n == CT - 1:
                    last.then_inc(glu_act, 1)

            def mix_pools(layer, first):
                pe.wait_ge(pooled_pe, 1)
                pe.sem_inc(pooled_pe, -1)
                if first:
                    pe.wait_ge(weights_in, 16 * 4 * (layer + 1))
                for g in range(CT):
                    last = nc.tensor.matmul(bank[:, 0, g * P:(g + 1) * P], wpool_sb[:, g, :], hT[:, CT + g, :],
                                            start=True, stop=True)
                last.then_inc(poolmix_dve, 1)

            def project_out(half, n, layer, first):
                if half == 1 and n == 0:
                    pe.wait_ge(mixB_pe, 1)
                    pe.sem_inc(mixB_pe, -1)
                    if first:
                        pe.wait_ge(wout_in, 16 * (layer + 1))
                dst = bank[:, 2 + n, :] if half == 1 else ff[:, n, :]
                for k in range(CT):
                    last = nc.tensor.matmul(dst, hT[:, half * CT + k, :], wout_sb[:, half * CT + k, n * 512:(n + 1) * 512],
                                            start=k == 0, stop=k == CT - 1)
                if half == 0 and n == 1:
                    last.then_inc(outA_dve, 1)

            def sums():
                pe.wait_ge(mixA_pe, 1)
                pe.sem_inc(mixA_pe, -1)
                for half, a in ((0, 512), (1, 1536)):
                    for k in range(CT):
                        last = nc.tensor.matmul(bank[:, 1, half:half + 1], work[:, a + k * P:a + (k + 1) * P], ones[:, :],
                                                start=k == 0, stop=k == CT - 1)
                last.then_inc(sums_dve, 1)

            def turn_h():
                pe.wait_ge(h_pe, 1)
                pe.sem_inc(h_pe, -1)
                for k in range(KD):
                    last = nc.tensor.transpose(bank[:, k // 4, (k % 4) * P:(k % 4 + 1) * P],
                                               h_next[:, k * P:(k + 1) * P], ident[:, :])
                last.then_inc(hT2_act, 1)

            def query(h, half):
                for k in range(KD):
                    last = nc.tensor.matmul(bank[:, 2 + h % 2, half * P:(half + 1) * P],
                                            wq_sb[:, k, (2 * h + half) * P:(2 * h + half + 1) * P], hT[:, k, :],
                                            start=k == 0, stop=k == KD - 1)
                if half == 1:
                    last.then_inc(q_act, 1)

            def scores(h, begin=False):
                pe.wait_ge(qT_pe, 1)
                pe.sem_inc(qT_pe, -1)
                if not begin:
                    pe.wait_ge(score_free_pe, 1)
                    pe.sem_inc(score_free_pe, -1)
                for half in range(2):
                    a = QT + 256 * (h % 2) + half * P
                    last = nc.tensor.matmul(ff[:, h % 2, half * P:(half + 1) * P], work[:, a:a + P], keys_sb[:, half, :],
                                            start=True, stop=True)
                last.then_inc(score_dve, 1)

            def step(f, layer_f, first, more):
                at = 0
                for h in range(2, HEADS):
                    c = (7 * (h - 2) + 1) // 2
                    choices(at, c)
                    query(h, 0)
                    choices(c, c + 1)
                    if h > 2:
                        scores(h - 1)
                    choices(c + 1, c + 2)
                    query(h, 1)
                    at = c + 2
                choices(at, 22)
                scores(HEADS - 1)
                if not more:
                    choices(22, CHOICES)
                    return
                if first:
                    choices(22, 28)
                    turn_maps()
                    turn_x()
                else:
                    choices(22, 24)
                    turn_x()
                    choices(24, 29)
                at = 28 if first else 29
                for m in range(KD):
                    c = 29 + (3 * m) // 2
                    choices(at, c)
                    project(f, m)
                    at = c
                choices(at, 43)
                state_inputs(0)
                at = 43
                for q in range(1, 4):
                    choices(at, 40 + 8 * q)
                    state_inputs(q)
                    choices(40 + 8 * q, 45 + 8 * q)
                    state_outputs(q - 1)
                    at = 45 + 8 * q
                choices(at, 75)
                state_outputs(3)
                choices(75, 80)
                mix_pools(layer_f, first)
                choices(80, 82)
                for n in range(CT):
                    glu(n)
                    choices(82 + n, 83 + n)
                project_out(1, 0, layer_f, first)
                choices(86, 88)
                project_out(1, 1, layer_f, first)
                choices(88, 90)
                sums()
                project_out(0, 0, layer_f, first)
                choices(90, 92)
                project_out(0, 1, layer_f, first)
                choices(92, 104)
                turn_h()
                choices(104, 106)
                if first:
                    pe.wait_ge(wq_in, 16 * (layer_f + 1))
                pe.wait_ge(hT2_pe, 1)
                pe.sem_inc(hT2_pe, -1)
                query(0, 0)
                query(0, 1)
                choices(106, 109)
                query(1, 0)
                query(1, 1)
                scores(0)
                choices(109, 112)
                scores(1)
                choices(112, CHOICES)

            pe.wait_ge(consts_pe, 1)
            pe.sem_inc(consts_pe, -1)
            pe.sem_inc(acc_free_pe, 1)
            turn_maps()
            turn_x()
            for m in range(KD):
                project(0, m)
            state_inputs(0)
            for q in range(1, 4):
                state_inputs(q)
                state_outputs(q - 1)
            state_outputs(3)
            for n in range(CT):
                glu(n)
            mix_pools(0, True)
            project_out(1, 0, 0, True)
            project_out(1, 1, 0, True)
            sums()
            project_out(0, 0, 0, True)
            project_out(0, 1, 0, True)
            turn_h()
            pe.wait_ge(hT2_pe, 1)
            pe.sem_inc(hT2_pe, -1)
            pe.wait_ge(wq_in, 16)
            for h in range(2):
                query(h, 0)
                query(h, 1)
                scores(h, begin=True)
            for layer in range(DEPTH):
                s0 = layer * TILES
                with pe.Fori(s0, s0 + TILES - 1) as s:
                    step(s + 1, layer, False, True)
                if layer + 1 < DEPTH:
                    step(s0 + TILES, layer + 1, True, True)
            step(None, None, False, False)

        @block.vector
        def _(dve):
            V = nc.vector

            def tt(o, a, b, op):
                return V.tensor_tensor(o, a, b, op)

            def choices(s, a, b):
                for k in range(a, b):
                    j = SLOT_OF[k]
                    dve.wait_ge(row_in[j], (s * TURNS[j] + TURN[k] + 1) * 16)
                    V.tensor_tensor_reduce(out=slots[j][:, 0:D], in0=slots[j][:, 0:D], in1=h_dot[:, :],
                                           scale=1.0, scalar=0.0, op0=ALU.mult, op1=ALU.add,
                                           accum_out=dots[:, k % DOTS:k % DOTS + 1]).then_inc(dot_act, 1)

            def mean_square(src, dst, n, width):
                V.tensor_scalar(stat[:, dst:dst + n], stat[:, src:src + n], 1.0 / width, EPS, ALU.mult, ALU.add).then_inc(dve_own, 1)
                dve.wait_ge(dve_own, 1)
                dve.sem_inc(dve_own, -1)
                dve.sem_inc(ms_pool, 1)

            def add_experts():
                dve.wait_ge(acc_dve, 1)
                dve.sem_inc(acc_dve, -1)
                tt(x_pend[:, :], x_pend[:, :], acc[:, :], ALU.add).then_inc(dve_own, 1)
                dve.wait_ge(dve_own, 1)
                dve.sem_inc(dve_own, -1)
                dve.sem_inc(acc_free_pe, 1)

            def handover():
                V.tensor_copy(h_dot[:, :], h_next[:, :]).then_inc(dve_own, 1)
                dve.wait_ge(dve_own, 1)
                dve.sem_inc(dve_own, -1)

            def setup(layer):
                dt, lr, th, r, sh, s1, c1, ar, ai, zr, zi, t = (small[:, i, :] for i in range(12))
                lam_re, lam_im = par[:, LAM_RE:LAM_RE + BLOCKS], par[:, LAM_IM:LAM_IM + BLOCKS]
                dve.wait_ge(set_dve, 1)
                dve.sem_inc(set_dve, -1)
                dve.wait_ge(par_in, 16 * (layer + 1))
                tt(lr, lam_re, dt, ALU.mult)
                tt(th, lam_im, dt, ALU.mult).then_inc(dve_own, 1)
                dve.wait_ge(dve_own, 1)
                dve.sem_inc(dve_own, -1)
                V.tensor_scalar(t, th, 1.0 / (2 * math.pi), ROUND, ALU.mult, ALU.add).then_inc(dve_own, 1)
                dve.wait_ge(dve_own, 1)
                dve.sem_inc(dve_own, -1)
                V.tensor_scalar(t, t, ROUND, None, ALU.subtract).then_inc(dve_own, 1)
                dve.wait_ge(dve_own, 1)
                dve.sem_inc(dve_own, -1)
                for part in (TWO_PI_1, TWO_PI_2, TWO_PI_3):
                    V.scalar_tensor_tensor(th, t, -part, th, ALU.mult, ALU.add).then_inc(dve_own, 1)
                    dve.wait_ge(dve_own, 1)
                    dve.sem_inc(dve_own, -1)
                V.tensor_scalar(th, th, PI_BELOW, -PI_BELOW, ALU.min, ALU.max).then_inc(dve_own, 1)
                dve.wait_ge(dve_own, 1)
                dve.sem_inc(dve_own, -1)
                dve.sem_inc(set_act, 1)
                dve.wait_ge(set_dve, 1)
                dve.sem_inc(set_dve, -1)
                tt(c1, sh, sh, ALU.mult).then_inc(dve_own, 1)
                dve.wait_ge(dve_own, 1)
                dve.sem_inc(dve_own, -1)
                V.tensor_scalar(c1, c1, -2.0, 1.0, ALU.mult, ALU.add).then_inc(dve_own, 1)
                dve.wait_ge(dve_own, 1)
                dve.sem_inc(dve_own, -1)
                tt(ar, r, c1, ALU.mult)
                tt(ai, r, s1, ALU.mult).then_inc(dve_own, 1)
                dve.wait_ge(dve_own, 1)
                dve.sem_inc(dve_own, -1)
                tt(t, lam_re, lam_re, ALU.mult)
                tt(sh, lam_im, lam_im, ALU.mult).then_inc(dve_own, 1)
                dve.wait_ge(dve_own, 1)
                dve.sem_inc(dve_own, -1)
                tt(t, t, sh, ALU.add).then_inc(dve_own, 1)
                dve.wait_ge(dve_own, 1)
                dve.sem_inc(dve_own, -1)
                V.reciprocal(t, t)
                V.tensor_scalar(ar, ar, 1.0, None, ALU.subtract).then_inc(dve_own, 1)
                dve.wait_ge(dve_own, 1)
                dve.sem_inc(dve_own, -1)
                tt(zr, ar, lam_re, ALU.mult)
                tt(sh, ai, lam_im, ALU.mult).then_inc(dve_own, 1)
                dve.wait_ge(dve_own, 1)
                dve.sem_inc(dve_own, -1)
                tt(zr, zr, sh, ALU.add).then_inc(dve_own, 1)
                dve.wait_ge(dve_own, 1)
                dve.sem_inc(dve_own, -1)
                tt(zi, ai, lam_re, ALU.mult)
                tt(sh, ar, lam_im, ALU.mult).then_inc(dve_own, 1)
                dve.wait_ge(dve_own, 1)
                dve.sem_inc(dve_own, -1)
                tt(zi, zi, sh, ALU.subtract).then_inc(dve_own, 1)
                dve.wait_ge(dve_own, 1)
                dve.sem_inc(dve_own, -1)
                tt(zr, zr, t, ALU.mult)
                tt(zi, zi, t, ALU.mult).then_inc(dve_own, 1)
                dve.wait_ge(dve_own, 1)
                dve.sem_inc(dve_own, -1)
                dve.wait_ge(bc_in, 16 * (layer + 1))
                raw = hT[:, :, :].rearrange("p a b -> p (a b)")
                b_re, b_im, c_re, c_im = (raw[:, i * BC:(i + 1) * BC].rearrange("p (b h) -> p b h", h=GROUP_CH)
                                          for i in range(4))
                bd = [h_next[:, i * 512:(i + 1) * 512].rearrange("p (b c) -> p b c", c=BLOCK_CH) for i in range(2)]
                flat = uT[:, :, :].rearrange("p a b -> p (a b)")
                t1 = flat[:, 0:BC].rearrange("p (b h) -> p b h", h=GROUP_CH)
                t2 = flat[:, BC:2 * BC].rearrange("p (b h) -> p b h", h=GROUP_CH)
                zrb = zr.unsqueeze(2).broadcast_to([P, BLOCKS, GROUP_CH])
                zib = zi.unsqueeze(2).broadcast_to([P, BLOCKS, GROUP_CH])
                V.memset(h_next[:, :], 0.0)
                V.memset(cw[0][:, :, :], 0.0)
                V.memset(cw[1][:, :, :], 0.0)
                for out_i, (p, q, op) in enumerate(((b_re, b_im, ALU.subtract), (b_im, b_re, ALU.add))):
                    tt(t1, p, zrb, ALU.mult)
                    tt(t2, q, zib, ALU.mult).then_inc(dve_own, 1)
                    dve.wait_ge(dve_own, 1)
                    dve.sem_inc(dve_own, -1)
                    for half in range(2):
                        rows, cols = slice(64 * half, 64 * half + 64), slice(16 * half, 16 * half + 16)
                        tt(bd[out_i][rows, :, cols], t1[rows], t2[rows], op).then_inc(dve_own, 1)
                        dve.wait_ge(dve_own, 1)
                        dve.sem_inc(dve_own, -1)
                dve.sem_inc(bd_pe, 1)
                for half in range(2):
                    rows, cols = slice(64 * half, 64 * half + 64), slice(16 * half, 16 * half + 16)
                    V.tensor_copy(cw[0][rows, :, cols], c_re[rows])
                    V.tensor_scalar(cw[1][rows, :, cols], c_im[rows], -1.0, None, ALU.mult).then_inc(dve_own, 1)
                    dve.wait_ge(dve_own, 1)
                    dve.sem_inc(dve_own, -1)
                V.tensor_copy(tab_c[:, :, 0:1], c1.unsqueeze(2))
                V.tensor_copy(tab_s[:, :, 0:1], s1.unsqueeze(2)).then_inc(dve_own, 1)
                dve.wait_ge(dve_own, 1)
                dve.sem_inc(dve_own, -1)
                pool_space = poolT[:, :, :].rearrange("p a b -> p (a b)")
                n = 1
                while n < HALF:
                    m1 = flat[:, 0:BLOCKS * n].rearrange("p (b n) -> p b n", n=n)
                    m2 = pool_space[:, 0:BLOCKS * n].rearrange("p (b n) -> p b n", n=n)
                    cn = tab_c[:, :, n - 1:n].broadcast_to([P, BLOCKS, n])
                    sn = tab_s[:, :, n - 1:n].broadcast_to([P, BLOCKS, n])
                    tt(m1, tab_c[:, :, 0:n], cn, ALU.mult)
                    tt(m2, tab_s[:, :, 0:n], sn, ALU.mult).then_inc(dve_own, 1)
                    dve.wait_ge(dve_own, 1)
                    dve.sem_inc(dve_own, -1)
                    tt(tab_c[:, :, n:2 * n], m1, m2, ALU.subtract).then_inc(dve_own, 1)
                    dve.wait_ge(dve_own, 1)
                    dve.sem_inc(dve_own, -1)
                    tt(m1, tab_c[:, :, 0:n], sn, ALU.mult)
                    tt(m2, tab_s[:, :, 0:n], cn, ALU.mult).then_inc(dve_own, 1)
                    dve.wait_ge(dve_own, 1)
                    dve.sem_inc(dve_own, -1)
                    tt(tab_s[:, :, n:2 * n], m1, m2, ALU.add).then_inc(dve_own, 1)
                    dve.wait_ge(dve_own, 1)
                    dve.sem_inc(dve_own, -1)
                    n *= 2
                dve.wait_ge(bdT_dve, 1)
                dve.sem_inc(bdT_dve, -1)
                for ri in range(2):
                    V.tensor_copy(bT[ri][:, :, :].rearrange("p a b -> p (a b)"), bank[:, ri, :])
                V.memset(state[:, :, :], 0.0).then_inc(dve_own, 1)
                dve.wait_ge(dve_own, 1)
                dve.sem_inc(dve_own, -1)

            def keep_x():
                dve.wait_ge(xpend_free_dve, 1)
                dve.sem_inc(xpend_free_dve, -1)
                V.tensor_copy(x_pend[:, :], x_front[:, :]).then_inc(dve_own, 1)
                dve.wait_ge(dve_own, 1)
                dve.sem_inc(dve_own, -1)
                dve.sem_inc(xfront_free_sp, 1)

            def square_x():
                dve.wait_ge(sq_dve, 1)
                dve.sem_inc(sq_dve, -1)
                mean_square(2, 0, 1, D)

            def halo(first):
                if first:
                    V.memset(poolT[:, :, 0:HALO], 0.0).then_inc(dve_own, 1)
                    dve.wait_ge(dve_own, 1)
                    dve.sem_inc(dve_own, -1)
                else:
                    V.tensor_copy(poolT[:, :, 0:HALO], poolT[:, :, P:P + HALO]).then_inc(dve_own, 1)
                    dve.wait_ge(dve_own, 1)
                    dve.sem_inc(dve_own, -1)
                dve.sem_inc(halo_act, 1)

            def normed(f):
                dve.wait_ge(rstd_dve, 1)
                dve.sem_inc(rstd_dve, -1)
                dve.wait_ge(x_in, 16 * (f + 1))
                V.tensor_scalar(h_next[:, :], x_front[:, :], stat[:, 1:2], None, ALU.mult).then_inc(xn_pe, 1)

            def turned_x():
                dve.wait_ge(hTp_dve, 1)
                dve.sem_inc(hTp_dve, -1)
                gain = par[:, G_MIX:G_MIX + KD].unsqueeze(2).broadcast_to([P, KD, P])
                tt(hT[:, :, :], bank[:, 0:2, :].rearrange("p a (b c) -> p (a b) c", c=P), gain, ALU.mult).then_inc(hT_pe, 1)

            def tabs(q):
                return [t[:, 4 * q:4 * q + 4, :].unsqueeze(2).broadcast_to([P, 4, 2, HALF]) for t in (tab_c, tab_s)]

            def spaces(q):
                a = (q % 2) * D
                return piece(a, 4, 2, HALF), piece(2048, 4, 2, HALF), piece(a + 512, 4, 2, HALF), piece(2560, 4, 2, HALF)

            def scan(q, half):
                re, re_out, im, im_out = spaces(q)
                for i in range(4):
                    b = 4 * q + i
                    decay = small[:, 3, b:b + 1].broadcast_to([P, HALF])
                    V.tensor_tensor_scan(re_out[:, i, half, :], decay, re[:, i, half, :], state[:, 0, b:b + 1],
                                         ALU.mult, ALU.add)
                    last = V.tensor_tensor_scan(im_out[:, i, half, :], decay, im[:, i, half, :], state[:, 1, b:b + 1],
                                                ALU.mult, ALU.add)
                last.then_inc(dve_own, 1)
                dve.wait_ge(dve_own, 1)
                dve.sem_inc(dve_own, -1)

            def turn_back(q):
                if q == 0:
                    dve.wait_ge(uT_dve, 1)
                    dve.sem_inc(uT_dve, -1)
                dve.wait_ge(bu_dve, 1)
                dve.sem_inc(bu_dve, -1)
                if q >= 2:
                    dve.wait_ge(s_used_dve, 1)
                    dve.sem_inc(s_used_dve, -1)
                A, B, C, E = spaces(q)
                tc, ts = tabs(q)
                re = bank[:, :, 0:P].rearrange("p i (h t) -> p i h t", h=2)
                im = bank[:, :, P:2 * P].rearrange("p i (h t) -> p i h t", h=2)
                tt(A, re, tc, ALU.mult)
                tt(B, im, ts, ALU.mult)
                tt(C, im, tc, ALU.mult)
                tt(E, re, ts, ALU.mult).then_inc(dve_own, 1)
                dve.wait_ge(dve_own, 1)
                dve.sem_inc(dve_own, -1)
                if q < 3:
                    dve.sem_inc(bu_free_pe, 1)

            def first_half(q):
                A, B, C, E = spaces(q)
                tt(A, A, B, ALU.add)
                tt(C, C, E, ALU.subtract).then_inc(dve_own, 1)
                dve.wait_ge(dve_own, 1)
                dve.sem_inc(dve_own, -1)
                scan(q, 0)
                c64, s64 = (t[:, 4 * q:4 * q + 4, HALF - 1] for t in (tab_c, tab_s))
                zr, zi = B[:, :, 0, HALF - 1], E[:, :, 0, HALF - 1]
                for n, (u, v) in enumerate(((zr, c64), (zi, s64), (zr, s64), (zi, c64))):
                    last = tt(hand[:, n, :], u, v, ALU.mult)
                last.then_inc(dve_own, 1)
                dve.wait_ge(dve_own, 1)
                dve.sem_inc(dve_own, -1)
                tt(state[:, 0, 4 * q:4 * q + 4], hand[:, 0, :], hand[:, 1, :], ALU.subtract)
                tt(state[:, 1, 4 * q:4 * q + 4], hand[:, 2, :], hand[:, 3, :], ALU.add).then_inc(dve_own, 1)
                dve.wait_ge(dve_own, 1)
                dve.sem_inc(dve_own, -1)

            def second_half(q):
                scan(q, 1)
                A, B, C, E = spaces(q)
                tc, ts = tabs(q)
                tt(A, tc, B, ALU.mult)
                tt(C, ts, E, ALU.mult).then_inc(dve_own, 1)
                dve.wait_ge(dve_own, 1)
                dve.sem_inc(dve_own, -1)

            def turn_forth(q):
                A, B, C, E = spaces(q)
                tc, ts = tabs(q)
                tt(A, A, C, ALU.subtract)
                tt(E, tc, E, ALU.mult)
                tt(B, ts, B, ALU.mult).then_inc(dve_own, 1)
                dve.wait_ge(dve_own, 1)
                dve.sem_inc(dve_own, -1)
                tt(C, E, B, ALU.add).then_inc(dve_own, 1)
                dve.wait_ge(dve_own, 1)
                dve.sem_inc(dve_own, -1)
                dve.sem_inc(s_pe, 1)
                V.tensor_copy(state[:, 0, 4 * q:4 * q + 4], A[:, :, 1, HALF - 1])
                V.tensor_copy(state[:, 1, 4 * q:4 * q + 4], C[:, :, 1, HALF - 1]).then_inc(dve_own, 1)
                dve.wait_ge(dve_own, 1)
                dve.sem_inc(dve_own, -1)

            def skip():
                tt(uT[:, :, :], uT[:, :, :], par[:, D_SKIP:D_SKIP + CT].unsqueeze(2).broadcast_to([P, CT, P]), ALU.mult).then_inc(dve_own, 1)
                dve.wait_ge(dve_own, 1)
                dve.sem_inc(dve_own, -1)

            def ssm_output():
                dve.wait_ge(y_dve, 1)
                dve.sem_inc(y_dve, -1)
                tt(uT[:, :, :], uT[:, :, :], ff[:, 0, :].rearrange("p (a b) -> p a b", a=CT), ALU.add).then_inc(y_act, 1)

            L = HALO + P
            sums = [poolT[:, :, :], piece(1024, CT, L), piece(1600, CT - 1, L), piece(2032, CT - 2, L), piece(2320, 1, L)]

            def windows():
                dve.wait_ge(poolT_dve, 1)
                dve.sem_inc(poolT_dve, -1)
                for n, w in enumerate(WINDOWS):
                    lag = w // 2
                    prev = sums[n] if n == 0 else sums[n][:, 1:, :]
                    tt(sums[n + 1][:, :, w - 1:], prev[:, :, w - 1:], prev[:, :, w - 1 - lag:L - lag], ALU.add).then_inc(dve_own, 1)
                    dve.wait_ge(dve_own, 1)
                    dve.sem_inc(dve_own, -1)

            def pooled(first):
                for n, w in enumerate(WINDOWS):
                    V.scalar_tensor_tensor(hT[:, CT + n, :], sums[n + 1][:, 0, HALO:], 1.0 / w, poolT[:, n, HALO:],
                                           ALU.mult, ALU.subtract).then_inc(dve_own, 1)
                    dve.wait_ge(dve_own, 1)
                    dve.sem_inc(dve_own, -1)
                    if first:
                        tt(sums[n + 1][:, 0, HALO:2 * HALO], sums[n + 1][:, 0, HALO:2 * HALO], invcnt[:, n, :], ALU.mult).then_inc(dve_own, 1)
                        dve.wait_ge(dve_own, 1)
                        dve.sem_inc(dve_own, -1)
                        tt(hT[:, CT + n, 0:HALO], sums[n + 1][:, 0, HALO:2 * HALO], poolT[:, n, HALO:2 * HALO], ALU.subtract).then_inc(dve_own, 1)
                        dve.wait_ge(dve_own, 1)
                        dve.sem_inc(dve_own, -1)
                dve.sem_inc(pooled_pe, 1)

            def pool_output():
                dve.wait_ge(poolmix_dve, 1)
                dve.sem_inc(poolmix_dve, -1)
                yp = piece(1024, CT, P)
                tt(yp, bank[:, 0, :].rearrange("p (a b) -> p a b", a=CT),
                   par[:, P_SCALE:P_SCALE + CT].unsqueeze(2).broadcast_to([P, CT, P]), ALU.mult).then_inc(dve_own, 1)
                dve.wait_ge(dve_own, 1)
                dve.sem_inc(dve_own, -1)
                tt(piece(1536, CT, P), yp, yp, ALU.mult)
                tt(hT[:, CT:2 * CT, :], yp, par[:, G_POOL:G_POOL + CT].unsqueeze(2).broadcast_to([P, CT, P]),
                   ALU.mult).then_inc(mixB_pe, 1)

            def gated():
                dve.wait_ge(sg_dve, 1)
                dve.sem_inc(sg_dve, -1)
                tt(uT[:, :, :], uT[:, :, :], piece(0, CT, P), ALU.mult).then_inc(dve_own, 1)
                dve.wait_ge(dve_own, 1)
                dve.sem_inc(dve_own, -1)
                tt(piece(512, CT, P), uT[:, :, :], uT[:, :, :], ALU.mult)
                tt(hT[:, 0:CT, :], uT[:, :, :], par[:, G_SSM:G_SSM + CT].unsqueeze(2).broadcast_to([P, CT, P]),
                   ALU.mult).then_inc(mixA_pe, 1)

            def head_squares():
                dve.wait_ge(sums_dve, 1)
                dve.sem_inc(sums_dve, -1)
                V.tensor_scalar(stat[:, 4:6], bank[:, 1, 0:2], 1.0 / SSM, EPS, ALU.mult, ALU.add).then_inc(dve_own, 1)
                dve.wait_ge(dve_own, 1)
                dve.sem_inc(dve_own, -1)
                dve.sem_inc(ms_pool, 1)

            def residual():
                dve.wait_ge(rstd_dve, 1)
                dve.sem_inc(rstd_dve, -1)
                dve.wait_ge(outA_dve, 1)
                dve.sem_inc(outA_dve, -1)
                V.scalar_tensor_tensor(x_front[:, :], ff[:, :, :].rearrange("p a b -> p (a b)"), stat[:, 6:7],
                                       x_front[:, :], ALU.mult, ALU.add).then_inc(dve_own, 1)
                dve.wait_ge(dve_own, 1)
                dve.sem_inc(dve_own, -1)
                V.scalar_tensor_tensor(x_front[:, :], bank[:, 2:4, :].rearrange("p a b -> p (a b)"), stat[:, 7:8],
                                       x_front[:, :], ALU.mult, ALU.add).then_inc(dve_own, 1)
                dve.wait_ge(dve_own, 1)
                dve.sem_inc(dve_own, -1)
                dve.sem_inc(xmid_act, 1)
                dve.sem_inc(mix_done_sp, 1)

            def square_mixed(layer, first):
                if first:
                    dve.wait_ge(weights_in, 16 * 4 * (layer + 1))
                dve.wait_ge(sq_dve, 1)
                dve.sem_inc(sq_dve, -1)
                mean_square(10, 8, 1, D)

            def normed_mixed():
                dve.wait_ge(rstd_dve, 1)
                dve.sem_inc(rstd_dve, -1)
                V.scalar_tensor_tensor(h_next[:, :], x_front[:, :], stat[:, 9:10], gffn_sb[:, :], ALU.mult, ALU.mult).then_inc(dve_own, 1)
                dve.wait_ge(dve_own, 1)
                dve.sem_inc(dve_own, -1)
                dve.sem_inc(h_pe, 1)

            def top_keys(h):
                dve.wait_ge(score_dve, 1)
                dve.sem_inc(score_dve, -1)
                sc = [ff[:, h % 2, side * KEYS:(side + 1) * KEYS] for side in range(2)]
                rest = [piece(REST + side * KEYS, KEYS) for side in range(2)]
                V.max(v16[:, 0, 0:8], sc[0])
                V.max(v16[:, 1, 0:8], sc[1]).then_inc(dve_own, 1)
                dve.wait_ge(dve_own, 1)
                dve.sem_inc(dve_own, -1)
                V.match_replace(rest[0], v16[:, 0, 0:8], sc[0], LOWEST)
                V.match_replace(rest[1], v16[:, 1, 0:8], sc[1], LOWEST)
                V.max_index(i12[:, h, 0, 0:8], v16[:, 0, 0:8], sc[0])
                V.max_index(i12[:, h, 1, 0:8], v16[:, 1, 0:8], sc[1]).then_inc(dve_own, 1)
                dve.wait_ge(dve_own, 1)
                dve.sem_inc(dve_own, -1)
                dve.sem_inc(score_free_pe, 1)
                V.max(v16[:, 0, 8:16], rest[0])
                V.max(v16[:, 1, 8:16], rest[1]).then_inc(dve_own, 1)
                dve.wait_ge(dve_own, 1)
                dve.sem_inc(dve_own, -1)

            def top_pairs(h):
                rest = [piece(REST + side * KEYS, KEYS) for side in range(2)]
                V.max_index(i12[:, h, 0, 8:16], v16[:, 0, 8:16], rest[0])
                V.max_index(i12[:, h, 1, 8:16], v16[:, 1, 8:16], rest[1])
                cand, left = piece(CAND, TOPK * TOPK), piece(LEFT, TOPK * TOPK)
                tt(piece(CAND, TOPK, TOPK), v16[:, 0, :].unsqueeze(2).broadcast_to([P, TOPK, TOPK]),
                   v16[:, 1, :].unsqueeze(1).broadcast_to([P, TOPK, TOPK]), ALU.add).then_inc(dve_own, 1)
                dve.wait_ge(dve_own, 1)
                dve.sem_inc(dve_own, -1)
                V.max(best[:, h, 0:8], cand).then_inc(dve_own, 1)
                dve.wait_ge(dve_own, 1)
                dve.sem_inc(dve_own, -1)
                V.max_index(sel[:, h, 0:8], best[:, h, 0:8], cand)
                V.match_replace(left, best[:, h, 0:8], cand, LOWEST).then_inc(dve_own, 1)
                dve.wait_ge(dve_own, 1)
                dve.sem_inc(dve_own, -1)
                V.max(best[:, h, 8:16], left).then_inc(dve_own, 1)
                dve.wait_ge(dve_own, 1)
                dve.sem_inc(dve_own, -1)
                V.max_index(sel[:, h, 8:16], best[:, h, 8:16], left).then_inc(dve_own, 1)
                dve.wait_ge(dve_own, 1)
                dve.sem_inc(dve_own, -1)

            def lookup(n, side):
                digit = piece(MISC, PAIR).bitcast(U32)
                digit_f, ids = piece(MISC + 32, PAIR), piece(MISC + 64, 2, TOPK)
                row = piece(MISC + 96 + side * PAIR, PAIR)
                chosen = sel[:, 2 * n:2 * n + 2, :].rearrange("p h k -> p (h k)")
                if side == 0:
                    V.tensor_scalar(digit, chosen, 4, None, ALU.logical_shift_right)
                else:
                    V.tensor_scalar(digit, chosen, TOPK - 1, None, ALU.bitwise_and)
                V.tensor_copy(ids, i12[:, 2 * n:2 * n + 2, side, :]).then_inc(dve_own, 1)
                dve.wait_ge(dve_own, 1)
                dve.sem_inc(dve_own, -1)
                V.tensor_copy(digit_f, digit).then_inc(dve_own, 1)
                dve.wait_ge(dve_own, 1)
                dve.sem_inc(dve_own, -1)
                hot = piece(HOT, PAIR, TOPK)
                tt(hot, digit_f.unsqueeze(2).broadcast_to([P, PAIR, TOPK]),
                   iota16[:, :].unsqueeze(1).broadcast_to([P, PAIR, TOPK]), ALU.is_equal).then_inc(dve_own, 1)
                dve.wait_ge(dve_own, 1)
                dve.sem_inc(dve_own, -1)
                hot4 = piece(HOT, 2, TOPK * TOPK).rearrange("p h (k c) -> p h k c", k=TOPK)
                tt(hot4, hot4, ids.unsqueeze(2).broadcast_to([P, 2, TOPK, TOPK]), ALU.mult).then_inc(dve_own, 1)
                dve.wait_ge(dve_own, 1)
                dve.sem_inc(dve_own, -1)
                V.tensor_reduce(row, hot, AX_X, ALU.add).then_inc(dve_own, 1)
                dve.wait_ge(dve_own, 1)
                dve.sem_inc(dve_own, -1)

            def first_ids(n):
                lookup(n, 0)
                g3 = gates[:, n * PAIR:(n + 1) * PAIR].rearrange("p (h k) -> p h k", h=2)
                tt(g3, best[:, 2 * n:2 * n + 2, :], best[:, 2 * n:2 * n + 2, 0:1].broadcast_to([P, 2, TOPK]), ALU.subtract).then_inc(dve_own, 1)
                dve.wait_ge(dve_own, 1)
                dve.sem_inc(dve_own, -1)
                dve.sem_inc(e_act, 1)

            def second_ids(n, layer):
                lookup(n, 1)
                row0, row1 = piece(MISC + 96, PAIR), piece(MISC + 96 + PAIR, PAIR)
                V.tensor_scalar(row0, row0, float(KEYS), float(layer * EXPERTS), ALU.mult, ALU.add).then_inc(dve_own, 1)
                dve.wait_ge(dve_own, 1)
                dve.sem_inc(dve_own, -1)
                tt(rows_of[:, n * PAIR:(n + 1) * PAIR], row0, row1, ALU.add).then_inc(dve_own, 1)
                dve.wait_ge(dve_own, 1)
                dve.sem_inc(dve_own, -1)
                dve.sem_inc(idx_pool, 1)
                dve.wait_ge(e_dve, 1)
                dve.sem_inc(e_dve, -1)
                g3 = gates[:, n * PAIR:(n + 1) * PAIR].rearrange("p (h k) -> p h k", h=2)
                V.tensor_reduce(hsum[:, :], g3, AX_X, ALU.add).then_inc(dve_own, 1)
                dve.wait_ge(dve_own, 1)
                dve.sem_inc(dve_own, -1)
                V.reciprocal(hsum[:, :], hsum[:, :]).then_inc(dve_own, 1)
                dve.wait_ge(dve_own, 1)
                dve.sem_inc(dve_own, -1)
                tt(g3, g3, hsum[:, :].unsqueeze(2).broadcast_to([P, 2, TOPK]), ALU.mult).then_inc(dve_own, 1)
                dve.wait_ge(dve_own, 1)
                dve.sem_inc(dve_own, -1)
                dve.sem_inc(gates_act, 1)

            def finished_tiles():
                dve.wait_ge(final_in, 16 * TILES)
                for t in range(TILES - 1):
                    V.tensor_tensor_reduce(out=final[4], in0=final[1 + t], in1=final[1 + t], scale=1.0, scalar=0.0,
                                           op0=ALU.mult, op1=ALU.add, accum_out=stat[:, 20 + t:21 + t]).then_inc(dve_own, 1)
                    dve.wait_ge(dve_own, 1)
                    dve.sem_inc(dve_own, -1)
                mean_square(20, 12, TILES - 1, D)

            def scale_finished():
                dve.wait_ge(rstd_dve, 1)
                dve.sem_inc(rstd_dve, -1)
                for t in range(TILES - 1):
                    V.scalar_tensor_tensor(final[1 + t], final[1 + t], stat[:, 15 + t:16 + t], final[0],
                                           ALU.mult, ALU.mult).then_inc(dve_own, 1)
                    dve.wait_ge(dve_own, 1)
                    dve.sem_inc(dve_own, -1)
                dve.sem_inc(final_sp, 1)

            def step(s, layer_s, f, layer_f, first, more):
                if more:
                    choices(s, 0, 3)
                    keep_x()
                    choices(s, 3, 6)
                else:
                    keep_x()
                    choices(s, 0, 6)
                top_keys(2)
                choices(s, 6, 8)
                top_pairs(2)
                choices(s, 8, 10)
                top_keys(3)
                if more:
                    choices(s, 10, 11)
                    square_x()
                    choices(s, 11, 12)
                else:
                    choices(s, 10, 12)
                top_pairs(3)
                choices(s, 12, 13)
                top_keys(4)
                choices(s, 13, 15)
                first_ids(1)
                choices(s, 15, 16)
                top_pairs(4)
                choices(s, 16, 17)
                top_keys(5)
                choices(s, 17, 19)
                second_ids(1, layer_s)
                if more and not first:
                    choices(s, 19, 20)
                    normed(f)
                    choices(s, 20, 21)
                else:
                    choices(s, 19, 21)
                top_pairs(5)
                choices(s, 21, 22)
                top_keys(6)
                choices(s, 22, 23)
                first_ids(2)
                choices(s, 23, 24)
                top_pairs(6)
                choices(s, 24, 25)
                top_keys(7)
                choices(s, 25, 26)
                second_ids(2, layer_s)
                choices(s, 26, 27)
                if more and not first:
                    turned_x()
                top_pairs(7)
                choices(s, 27, 29)
                first_ids(3)
                choices(s, 29, 31)
                second_ids(3, layer_s)
                dve.sem_inc(front_done_sp, 1)
                if not more:
                    choices(s, 31, 60)
                    finished_tiles()
                    choices(s, 60, 66)
                    scale_finished()
                    choices(s, 66, CHOICES)
                    return
                if first:
                    setup(layer_f)
                    halo(True)
                    normed(f)
                    turned_x()
                else:
                    halo(False)
                choices(s, 31, 44)
                for q in range(4):
                    c = 44 + 8 * q
                    turn_back(q)
                    choices(s, c, c + 2)
                    first_half(q)
                    choices(s, c + 2, c + 4)
                    second_half(q)
                    choices(s, c + 4, c + 6)
                    turn_forth(q)
                    if q < 3:
                        choices(s, c + 6, c + 8)
                choices(s, 74, 75)
                skip()
                choices(s, 75, 78)
                ssm_output()
                windows()
                choices(s, 78, 79)
                pooled(first)
                choices(s, 79, 84)
                pool_output()
                choices(s, 84, 88)
                gated()
                choices(s, 88, 92)
                head_squares()
                choices(s, 92, 97)
                residual()
                choices(s, 97, 100)
                square_mixed(layer_f, first)
                choices(s, 100, 103)
                normed_mixed()
                choices(s, 103, 112)
                top_keys(0)
                choices(s, 112, 114)
                top_pairs(0)
                choices(s, 114, 116)
                top_keys(1)
                choices(s, 116, 117)
                top_pairs(1)
                choices(s, 117, 119)
                first_ids(0)
                choices(s, 119, 121)
                second_ids(0, layer_f)
                choices(s, 121, CHOICES)

            dve.wait_ge(consts_dve, 1)
            dve.sem_inc(consts_dve, -1)
            for n, w in enumerate(WINDOWS):
                V.tensor_scalar(invcnt[:, n, :], iota16[:, :], 1.0, float(w), ALU.add, ALU.min).then_inc(dve_own, 1)
                dve.wait_ge(dve_own, 1)
                dve.sem_inc(dve_own, -1)
            V.reciprocal(invcnt[:, :, :], invcnt[:, :, :]).then_inc(dve_own, 1)
            dve.wait_ge(dve_own, 1)
            dve.sem_inc(dve_own, -1)
            square_x()
            setup(0)
            halo(True)
            normed(0)
            turned_x()
            for q in range(4):
                turn_back(q)
                first_half(q)
                second_half(q)
                turn_forth(q)
            skip()
            ssm_output()
            windows()
            pooled(True)
            pool_output()
            gated()
            head_squares()
            residual()
            square_mixed(0, True)
            normed_mixed()
            for h in range(2):
                top_keys(h)
                top_pairs(h)
            first_ids(0)
            second_ids(0, 0)
            handover()
            for layer in range(DEPTH):
                s0 = layer * TILES
                with dve.Fori(s0, s0 + TILES - 1) as s:
                    step(s, layer, s + 1, layer, False, True)
                    add_experts()
                    dve.sem_inc(out_sp, 1)
                    handover()
                if layer + 1 < DEPTH:
                    step(s0 + TILES - 1, layer, s0 + TILES, layer + 1, True, True)
                    add_experts()
                    dve.sem_inc(out_sp, 1)
                    handover()
            step(STEPS - 1, DEPTH - 1, None, None, False, False)
            add_experts()
            V.tensor_tensor_reduce(out=h_dot[:, :], in0=x_pend[:, :], in1=x_pend[:, :], scale=1.0,
                                   scalar=0.0, op0=ALU.mult, op1=ALU.add, accum_out=stat[:, 23:24]).then_inc(dve_own, 1)
            dve.wait_ge(dve_own, 1)
            dve.sem_inc(dve_own, -1)
            mean_square(23, 18, 1, D)
            dve.wait_ge(rstd_dve, 1)
            dve.sem_inc(rstd_dve, -1)
            V.scalar_tensor_tensor(x_pend[:, :], x_pend[:, :], stat[:, 19:20], final[0], ALU.mult, ALU.mult).then_inc(dve_own, 1)
            dve.wait_ge(dve_own, 1)
            dve.sem_inc(dve_own, -1)
            dve.sem_inc(out_sp, 1)


def kernel(x, norm_mix, w_in, a_re, a_im, log_dt, b_re, b_im, c_re, c_im, d_skip, w_glu, b_glu, w_pool,
           pool_scale, g_out_ssm, g_out_pool, w_out, norm_ffn, w_q, k1, k2, u_experts, v_experts, norm_final):
    import numpy as np
    import concourse.bacc as bacc
    from concourse.bass_utils import run_bass_kernel_spmd as run

    (x, norm_mix, w_in, a_re, a_im, log_dt, b_re, b_im, c_re, c_im, d_skip, w_glu, b_glu, w_pool, pool_scale,
     g_out_ssm, g_out_pool, w_out, norm_ffn, w_q, k1, k2, u_experts, v_experts, norm_final) = (
        np.asarray(a) for a in (x, norm_mix, w_in, a_re, a_im, log_dt, b_re, b_im, c_re, c_im, d_skip, w_glu, b_glu,
                                w_pool, pool_scale, g_out_ssm, g_out_pool, w_out, norm_ffn, w_q, k1, k2, u_experts,
                                v_experts, norm_final))

    def rows(w, k):
        l, d, n = w.shape
        return w.reshape(l, k, d // k, n).transpose(0, 2, 1, 3)

    def states(a):
        return a.reshape(DEPTH, BLOCKS, P).transpose(0, 2, 1)

    def channels(a, k):
        return a.reshape(DEPTH, k, P).transpose(0, 2, 1)

    def maps(a):
        return a.reshape(DEPTH, BLOCKS, P, GROUP_CH).transpose(0, 2, 1, 3).reshape(DEPTH, P, BC)

    arrays = {
        "x": x.reshape(SEQ, D),
        "win": w_in.reshape(DEPTH, KD, P, KD, P).transpose(0, 3, 2, 1, 4),
        "wout": rows(w_out, KD),
        "wglu": rows(w_glu, CT),
        "wpool": w_pool.transpose(0, 2, 1, 3),
        "wq": rows(w_q, KD),
        "keys": np.stack([k1.transpose(0, 2, 1), k2.transpose(0, 2, 1)], axis=2),
        "params": np.concatenate([
            states(a_re), states(a_im), states(np.repeat(log_dt, STATE, axis=1)), channels(norm_mix, KD),
            channels(d_skip, CT), channels(b_glu, CT), channels(pool_scale, CT), channels(g_out_ssm, CT),
            channels(g_out_pool, CT)], axis=2),
        "bc": np.concatenate([maps(b_re), maps(b_im), maps(c_re.transpose(0, 1, 3, 2)),
                              maps(c_im.transpose(0, 1, 3, 2))], axis=2),
        "gffn": np.repeat(norm_ffn[:, None, :], P, axis=1),
        "gfinal": np.repeat(norm_final[None, :], P, axis=0),
        "uv": np.concatenate([u_experts, v_experts], axis=2).reshape(DEPTH * EXPERTS, 2 * D),
    }
    nc = bacc.Bacc("TRN2", target_bir_lowering=False, num_devices=1, dynamic_dma_scratch_size=4096)
    in_map, args = {}, []
    for name, a in arrays.items():
        a = np.ascontiguousarray(a)
        in_map[f"{name}_dram"] = a
        args.append(nc.dram_tensor(f"{name}_dram", a.shape, F32, kind="ExternalInput").ap())
    args.append(nc.dram_tensor("x_state_dram", (SEQ, D), F32, kind="Internal").ap())
    args.append(nc.dram_tensor("out_dram", (SEQ, D), F32, kind="ExternalOutput").ap())
    build(nc, *args)
    r = run(nc, [in_map], core_ids=[0])
    return r.results[0]["out_dram"].reshape(1, SEQ, D)
```

```python
import math
from contextlib import ExitStack

import concourse.bass as bass
from concourse import mybir

F32 = mybir.dt.float32
I32 = mybir.dt.int32
U32 = mybir.dt.uint32
ALU = mybir.AluOpType
ACT = mybir.ActivationFunctionType
AX_X = mybir.AxisListType.X

P = 128
D = 1024
SEQ = 512
DEPTH = 2
TILES = SEQ // P
STEPS = DEPTH * TILES
KD = D // P
SSM = D // 2
CT = SSM // P
GROUP_CH = 16
STATE = 64
BLOCKS = (SSM // GROUP_CH) * STATE // P
BLOCK_CH = 2 * GROUP_CH
HALF = P // 2
WINDOWS = (2, 4, 8, 16)
HALO = 16
L = HALO + P
HEADS = 8
KEYS = 128
TOPK = 16
CHOICES = HEADS * TOPK
EXPERTS = KEYS * KEYS
EPS = 1e-6
PAIRS = HEADS // 2
PAIR = 2 * TOPK
SLOTS = 6
WIN_SLOTS = 3
DIAGS = 4
DOTS = 8
LOWEST = -3.0e38
ROUND = 12582912.0
TWO_PI_1 = 6.28125
TWO_PI_2 = 0.0019350051879882812
TWO_PI_3 = 2 * math.pi - TWO_PI_1 - TWO_PI_2
PI_BELOW = 3.1415925

REST, CAND, MISC = 2048, 2304, 2816
HOT, LEFT = CAND, REST

LAM_RE, LAM_IM, LOG_DT = 0, BLOCKS, 2 * BLOCKS
G_MIX = 3 * BLOCKS
D_SKIP = G_MIX + KD
B_GLU = D_SKIP + CT
P_SCALE = B_GLU + CT
G_SSM = P_SCALE + CT
G_POOL = G_SSM + CT
PARAMS = G_POOL + CT
BC = BLOCKS * GROUP_CH

DVE_SUMS = (82, 84, 86, 88)
SUM_LAG = 1
DIAG_OF = {k: n % DIAGS for n, k in enumerate(k for k in range(CHOICES) if k not in DVE_SUMS)}


def slot_plan():
    short = 0
    while (CHOICES - short * (SLOTS - 2)) % SLOTS:
        short += 1
    full = (CHOICES - short * (SLOTS - 2)) // SLOTS
    rounds = [SLOTS] * (full - full // 4) + [SLOTS - 2] * short + [SLOTS] * (full // 4)
    slot_of = [j for n in rounds for j in range(n)]
    last = {j: j - SLOTS for j in range(SLOTS)}
    taken, by_pe, by_dve, turn, turns = -SLOTS, [], [], [], [0] * SLOTS
    for k, j in enumerate(slot_of):
        freed = range(taken, max(taken, last[j] + 1))
        by_dve.append(sum(c in DVE_SUMS for c in freed))
        by_pe.append(len(freed) - by_dve[-1])
        taken = freed.stop
        last[j] = k
        turn.append(turns[j])
        turns[j] += 1
    return slot_of, turn, turns, by_pe, by_dve


SLOT_OF, TURN, TURNS, FREED, FREED_DVE = slot_plan()


def build(nc, x, win, wout, wglu, wpool, wq, keys, params, bc, gffn, gfinal, uv, x_state, out):
    ctx = ExitStack()
    with ctx:
        def sb(name, shape, dt=F32):
            return ctx.enter_context(nc.sbuf_tensor(name, shape, dt))

        def sem(name):
            return ctx.enter_context(nc.semaphore(name))

        wq_sb = sb("wq_sb", [P, KD, 2 * HEADS * KEYS])
        wout_sb = sb("wout_sb", [P, KD, D])
        wglu_sb = sb("wglu_sb", [P, CT, SSM])
        wpool_sb = sb("wpool_sb", [P, CT, P])
        keys_sb = sb("keys_sb", [P, 2, KEYS])
        par = sb("par", [P, PARAMS])
        gffn_sb = sb("gffn_sb", [P, D])
        slots = [sb(f"slot{j}", [P, 2 * D]) for j in range(SLOTS)]
        h_dot = sb("h_dot", [P, D])
        rows_of = sb("rows_of", [P, CHOICES], I32)
        gates = sb("gates", [P, CHOICES])
        dots = sb("dots", [P, DOTS])
        gelu_sb = sb("gelu_sb", [P, DOTS])
        diag = sb("diag", [P, DIAGS, P])
        x_pend = sb("x_pend", [P, D])
        x_front = sb("x_front", [P, D])
        h_next = sb("h_next", [P, D])
        hT = sb("hT", [P, KD, P])
        uT = sb("uT", [P, CT, P])
        poolT = sb("poolT", [P, CT, L])
        work = sb("work", [P, 3 * D])
        tab = sb("tab", [P, 2, BLOCKS, HALF])
        tab_c, tab_s = tab[:, 0], tab[:, 1]
        bT = [sb("bT_re", [P, CT, P]), sb("bT_im", [P, CT, P])]
        cw = [sb("cw_re", [P, BLOCKS, BLOCK_CH]), sb("cw_im", [P, BLOCKS, BLOCK_CH])]
        state = sb("state", [P, 2, BLOCKS])
        small = sb("small", [P, 12, BLOCKS])
        hand = sb("hand", [P, 4, 4])
        stat = sb("stat", [P, 24])
        v16 = sb("v16", [P, 2, TOPK])
        best = sb("best", [P, HEADS, TOPK])
        sel = sb("sel", [P, HEADS, TOPK], U32)
        i12 = sb("i12", [P, HEADS, 2, TOPK], U32)
        hsum = sb("hsum", [P, HEADS - 2])
        ident = sb("ident", [P, P])
        ones = sb("ones", [P, 1])
        mhalf = sb("mhalf", [P, TILES - 1])
        iota16 = sb("iota16", [P, TOPK])
        invcnt = sb("invcnt", [P, CT, HALO])

        acc = ctx.enter_context(nc.psum_tensor("acc", [P, D], F32))
        bank = ctx.enter_context(nc.psum_tensor("bank", [P, 4, 512], F32))
        ff = ctx.enter_context(nc.psum_tensor("ff", [P, 2, 512], F32))

        win_sb = [work[:, i * D:(i + 1) * D].rearrange("p (k n) -> p k n", k=KD) for i in range(WIN_SLOTS)]

        def piece(a, *shape):
            n = math.prod(shape)
            v = work[:, a:a + n]
            if len(shape) == 2:
                return v.rearrange("p (a b) -> p a b", a=shape[0])
            if len(shape) == 3:
                return v.rearrange("p (a b c) -> p a b c", a=shape[0], b=shape[1])
            return v

        def q_part(head):
            flat = uT[:, :, :].rearrange("p a b -> p (a b)")
            return flat[:, 256 * (head % 2):256 * (head % 2 + 1)]

        final_in = sem("final_in")
        par_in = sem("par_in")
        bc_in = sem("bc_in")
        weights_in = sem("weights_in")
        wout_in = sem("wout_in")
        wq_in = sem("wq_in")
        x_in = sem("x_in")
        win_in = [sem(f"win_in{i}") for i in range(WIN_SLOTS)]
        row_in = [sem(f"row_in{j}") for j in range(SLOTS)]
        x_stored = sem("x_stored")
        out_stored = sem("out_stored")
        dve_own = sem("dve_own")
        act_own = sem("act_own")
        pool_own = sem("pool_own")
        consts_pe = sem("consts_pe")
        consts_act = sem("consts_act")
        consts_dve = sem("consts_dve")
        slot_free_pool = sem("slot_free_pool")
        slot_free_by_dve_pool = sem("slot_free_by_dve_pool")
        scale_dve = sem("scale_dve")
        idx_pool = sem("idx_pool")
        dot_act = sem("dot_act")
        gates_act = sem("gates_act")
        diag_pe = sem("diag_pe")
        diag_free_act = sem("diag_free_act")
        acc_dve = sem("acc_dve")
        mix_done_sp = sem("mix_done_sp")
        final_sp = sem("final_sp")
        acc_free_pe = sem("acc_free_pe")
        out_sp = sem("out_sp")
        sq_dve = sem("sq_dve")
        ms_pool = sem("ms_pool")
        rstd_dve = sem("rstd_dve")
        rstd_act = sem("rstd_act")
        xn_pe = sem("xn_pe")
        hTp_dve = sem("hTp_dve")
        hT_pe = sem("hT_pe")
        win_used_sp = sem("win_used_sp")
        projA_act = sem("projA_act")
        projB_act = sem("projB_act")
        halo_act = sem("halo_act")
        uT_pe = sem("uT_pe")
        uT_dve = sem("uT_dve")
        poolT_dve = sem("poolT_dve")
        poolT_pe = sem("poolT_pe")
        bu_dve = sem("bu_dve")
        bu_free_pe = sem("bu_free_pe")
        s_pe = sem("s_pe")
        s_used_dve = sem("s_used_dve")
        sums_dve = sem("sums_dve")
        y_dve = sem("y_dve")
        y_act = sem("y_act")
        y1_pe = sem("y1_pe")
        glu_act = sem("glu_act")
        sg_dve = sem("sg_dve")
        mixA_pe = sem("mixA_pe")
        pooled_pe = sem("pooled_pe")
        poolmix_dve = sem("poolmix_dve")
        mixB_pe = sem("mixB_pe")
        outA_dve = sem("outA_dve")
        xmid_act = sem("xmid_act")
        h_pe = sem("h_pe")
        hT2_act = sem("hT2_act")
        hT2_pe = sem("hT2_pe")
        q_act = sem("q_act")
        qT_pe = sem("qT_pe")
        score_dve = sem("score_dve")
        score_free_pe = sem("score_free_pe")
        e_act = sem("e_act")
        e_dve = sem("e_dve")
        front_done_sp = sem("front_done_sp")
        xfront_free_sp = sem("xfront_free_sp")
        xpend_free_act = sem("xpend_free_act")
        set_act = sem("set_act")
        set_dve = sem("set_dve")
        bd_pe = sem("bd_pe")
        maps_pe = sem("maps_pe")
        bdT_dve = sem("bdT_dve")

        block = ctx.enter_context(nc.Block())
        final = [wq_sb[:, i, 0:D] for i in range(5)]

        @block.sync
        def _(sp):
            def load_win(m, layer):
                sp.dma_start(win_sb[m % WIN_SLOTS], win[layer, m]).then_inc(win_in[m % WIN_SLOTS], 16)

            def loads(f, layer, first, begin=False):
                if not begin:
                    sp.wait_ge(mix_done_sp, 1)
                    sp.sem_inc(mix_done_sp, -1)
                    sp.wait_ge(xfront_free_sp, 1)
                    sp.sem_inc(xfront_free_sp, -1)
                src = x_state if layer else x
                row = (f - layer * TILES) * P
                sp.dma_start(x_front[:, :], src[bass.ds(row, P), :]).then_inc(x_in, 16)
                if first:
                    sp.dma_start(par[:, :], params[layer]).then_inc(par_in, 16)
                load_win(0, layer)
                load_win(1, layer)
                if first:
                    sp.dma_start(tab_c[:, :, :].rearrange("p a b -> p (a b)"), bc[layer]).then_inc(bc_in, 16)
                if not begin:
                    sp.wait_ge(front_done_sp, 1)
                    sp.sem_inc(front_done_sp, -1)
                load_win(2, layer)
                if first:
                    sp.dma_start(wglu_sb[:, :, :], wglu[layer]).then_inc(weights_in, 16)
                    sp.dma_start(wpool_sb[:, :, :], wpool[layer]).then_inc(weights_in, 16)
                    sp.dma_start(keys_sb[:, :, :], keys[layer]).then_inc(weights_in, 16)
                    sp.dma_start(gffn_sb[:, :], gffn[layer]).then_inc(weights_in, 16)
                for m in range(WIN_SLOTS, KD):
                    sp.wait_ge(win_used_sp, 1)
                    sp.sem_inc(win_used_sp, -1)
                    load_win(m, layer)
                if first:
                    sp.dma_start(wout_sb[:, :, :], wout[layer]).then_inc(wout_in, 16)
                    sp.dma_start(wq_sb[:, :, :], wq[layer]).then_inc(wq_in, 16)

            def store(s, layer):
                sp.wait_ge(out_sp, 1)
                sp.sem_inc(out_sp, -1)
                row = (s - layer * TILES) * P
                sp.dma_start(x_state[bass.ds(row, P), :], x_pend[:, :]).then_inc(x_stored, 16)
                sp.wait_ge(x_stored, (s + 1) * 16)
                sp.sem_inc(xpend_free_act, 1)

            sp.sem_inc(xpend_free_act, 1)
            loads(0, 0, True, begin=True)
            for layer in range(DEPTH):
                s0 = layer * TILES
                with sp.Fori(s0, s0 + TILES - 1) as s:
                    loads(s + 1, layer, False)
                    store(s, layer)
                if layer + 1 < DEPTH:
                    loads(s0 + TILES, layer + 1, True)
                    store(s0 + TILES - 1, layer)
            sp.wait_ge(mix_done_sp, 1)
            sp.sem_inc(mix_done_sp, -1)
            sp.wait_ge(xfront_free_sp, 1)
            sp.sem_inc(xfront_free_sp, -1)
            sp.wait_ge(front_done_sp, 1)
            sp.sem_inc(front_done_sp, -1)
            sp.dma_start(final[0], gfinal).then_inc(final_in, 16)
            for t in range(TILES - 1):
                sp.dma_start(final[1 + t], x_state[t * P:(t + 1) * P, :]).then_inc(final_in, 16)
            sp.wait_ge(final_sp, 1)
            sp.sem_inc(final_sp, -1)
            for t in range(TILES - 1):
                sp.dma_start(out[t * P:(t + 1) * P, :], final[1 + t]).then_inc(out_stored, 16)
            sp.wait_ge(out_sp, 1)
            sp.sem_inc(out_sp, -1)
            sp.dma_start(out[(TILES - 1) * P:TILES * P, :], x_pend[:, :]).then_inc(out_stored, 16)
            sp.wait_ge(out_stored, 16 * TILES)

        @block.gpsimd
        def _(pool):
            def power(a, n):
                pool.wait_ge(ms_pool, 1)
                pool.sem_inc(ms_pool, -1)
                nc.gpsimd.tensor_tensor(stat[:, a + n:a + 2 * n], stat[:, a:a + n], mhalf[:, 0:n],
                                        ALU.pow).then_inc(rstd_dve, 1)

            def power_x():
                pool.wait_ge(ms_pool, 1)
                pool.sem_inc(ms_pool, -1)
                nc.gpsimd.tensor_tensor(stat[:, 1:2], stat[:, 0:1], mhalf[:, 0:1], ALU.pow).then_inc(rstd_act, 1)

            def choices(a, b):
                for k in range(a, b):
                    if k % PAIR == 0:
                        pool.wait_ge(idx_pool, 1)
                        pool.sem_inc(idx_pool, -1)
                    if FREED[k]:
                        pool.wait_ge(slot_free_pool, FREED[k])
                        pool.sem_inc(slot_free_pool, -FREED[k])
                    if FREED_DVE[k]:
                        pool.wait_ge(slot_free_by_dve_pool, FREED_DVE[k])
                        pool.sem_inc(slot_free_by_dve_pool, -FREED_DVE[k])
                    nc.gpsimd.indirect_dma_start(
                        out=slots[SLOT_OF[k]][:, :], out_offset=None, in_=uv[:, :],
                        in_offset=bass.IndirectOffsetOnAxis(ap=rows_of[:, k:k + 1], axis=0),
                    ).then_inc(row_in[SLOT_OF[k]], 16)

            def step(more):
                if more:
                    choices(0, 17)
                    power_x()
                    choices(17, 95)
                    power(4, 2)
                    choices(95, 101)
                    power(8, 1)
                    choices(101, CHOICES)
                else:
                    choices(0, 64)
                    power(12, TILES - 1)
                    choices(64, CHOICES)

            nc.gpsimd.memset(ident[:, :], 0.0).then_inc(pool_own, 1)
            pool.wait_ge(pool_own, 1)
            pool.sem_inc(pool_own, -1)
            nc.gpsimd.affine_select(out=ident[:, :], in_=ident[:, :], compare_op=ALU.not_equal, fill=1.0,
                                    base=0, pattern=[[-1, P]], channel_multiplier=1)
            nc.gpsimd.memset(ones[:, :], 1.0)
            nc.gpsimd.memset(mhalf[:, :], -0.5)
            nc.gpsimd.iota(iota16[:, :], pattern=[[1, TOPK]], base=0, channel_multiplier=0,
                           allow_small_or_imprecise_dtypes=True).then_inc(pool_own, 1)
            pool.wait_ge(pool_own, 1)
            pool.sem_inc(pool_own, -1)
            pool.sem_inc(consts_pe, 1)
            pool.sem_inc(consts_act, 1)
            pool.sem_inc(consts_dve, 1)
            pool.sem_inc(slot_free_pool, SLOTS)
            power_x()
            power(4, 2)
            power(8, 1)
            for layer in range(DEPTH):
                s0 = layer * TILES
                with pool.Fori(s0, s0 + TILES - 1):
                    step(True)
                if layer + 1 < DEPTH:
                    step(True)
            step(False)
            power(18, 1)

        @block.scalar
        def _(act):
            def choices(a, b):
                for k in range(a, b):
                    d = k % DOTS
                    if k % PAIR == 0:
                        act.wait_ge(gates_act, 1)
                        act.sem_inc(gates_act, -1)
                    act.wait_ge(dot_act, 1)
                    act.sem_inc(dot_act, -1)
                    nc.scalar.activation(gelu_sb[:, d:d + 1], dots[:, d:d + 1], ACT.Gelu).then_inc(act_own, 1)
                    act.wait_ge(act_own, 1)
                    act.sem_inc(act_own, -1)
                    nc.scalar.activation(dots[:, d:d + 1], gelu_sb[:, d:d + 1], ACT.Copy,
                                         scale=gates[:, k:k + 1]).then_inc(act_own, 1)
                    act.wait_ge(act_own, 1)
                    act.sem_inc(act_own, -1)
                    if k in DVE_SUMS:
                        act.sem_inc(scale_dve, 1)
                        continue
                    act.wait_ge(diag_free_act, 1)
                    act.sem_inc(diag_free_act, -1)
                    nc.scalar.activation(diag[:, DIAG_OF[k], :], ident[:, :], ACT.Copy,
                                         scale=dots[:, d:d + 1]).then_inc(diag_pe, 1)

            def step_sizes(layer):
                act.wait_ge(par_in, 16 * (layer + 1))
                nc.scalar.activation(small[:, 0, :], par[:, LOG_DT:LOG_DT + BLOCKS], ACT.Exp).then_inc(set_dve, 1)

            def sines():
                act.wait_ge(set_act, 1)
                act.sem_inc(set_act, -1)
                nc.scalar.activation(small[:, 3, :], small[:, 1, :], ACT.Exp).then_inc(act_own, 1)
                act.wait_ge(act_own, 1)
                act.sem_inc(act_own, -1)
                nc.scalar.activation(small[:, 4, :], small[:, 2, :], ACT.Sin, scale=0.5)
                nc.scalar.activation(small[:, 5, :], small[:, 2, :], ACT.Sin).then_inc(set_dve, 1)

            def square_x(f):
                act.wait_ge(x_in, 16 * (f + 1))
                nc.scalar.activation(h_next[:, :], x_front[:, :], ACT.Square, accum_out=stat[:, 2:3]).then_inc(sq_dve, 1)

            def keep_x():
                act.wait_ge(xpend_free_act, 1)
                act.sem_inc(xpend_free_act, -1)
                nc.scalar.activation(x_pend[:, :], x_front[:, :], ACT.Copy).then_inc(act_own, 1)
                act.wait_ge(act_own, 1)
                act.sem_inc(act_own, -1)
                act.sem_inc(xfront_free_sp, 1)

            def normed():
                act.wait_ge(rstd_act, 1)
                act.sem_inc(rstd_act, -1)
                nc.scalar.activation(h_next[:, :], x_front[:, :], ACT.Copy, scale=stat[:, 1:2]).then_inc(xn_pe, 1)

            def ssm_input():
                act.wait_ge(projA_act, 1)
                act.sem_inc(projA_act, -1)
                nc.scalar.activation(uT[:, :, :], bank[:, 2, :].rearrange("p (a b) -> p a b", a=CT),
                                     ACT.Copy).then_inc(act_own, 1)
                act.wait_ge(act_own, 1)
                act.sem_inc(act_own, -1)
                act.sem_inc(uT_pe, 1)
                act.sem_inc(uT_dve, 1)

            def pool_input():
                act.wait_ge(projB_act, 1)
                act.sem_inc(projB_act, -1)
                act.wait_ge(halo_act, 1)
                act.sem_inc(halo_act, -1)
                nc.scalar.activation(poolT[:, :, HALO:], bank[:, 3, :].rearrange("p (a b) -> p a b", a=CT),
                                     ACT.Copy).then_inc(act_own, 1)
                act.wait_ge(act_own, 1)
                act.sem_inc(act_own, -1)
                act.sem_inc(poolT_dve, 1)
                act.sem_inc(poolT_pe, 1)

            def gelu_y():
                act.wait_ge(y_act, 1)
                act.sem_inc(y_act, -1)
                nc.scalar.activation(uT[:, :, :], uT[:, :, :], ACT.Gelu).then_inc(y1_pe, 1)

            def glu_gate():
                act.wait_ge(glu_act, 1)
                act.sem_inc(glu_act, -1)
                for n in range(CT):
                    last = nc.scalar.activation(piece(n * P, P), ff[:, 1, n * P:(n + 1) * P], ACT.Sigmoid,
                                                bias=par[:, B_GLU + n:B_GLU + n + 1])
                last.then_inc(sg_dve, 1)

            def square_mixed():
                act.wait_ge(xmid_act, 1)
                act.sem_inc(xmid_act, -1)
                nc.scalar.activation(h_next[:, :], x_front[:, :], ACT.Square, accum_out=stat[:, 10:11]).then_inc(sq_dve, 1)

            def h_turned():
                act.wait_ge(hT2_act, 1)
                act.sem_inc(hT2_act, -1)
                nc.scalar.activation(hT[:, :, :].rearrange("p a b -> p (a b)"),
                                     bank[:, 0:2, :].rearrange("p a b -> p (a b)"), ACT.Copy).then_inc(hT2_pe, 1)

            def query(h):
                act.wait_ge(q_act, 1)
                act.sem_inc(q_act, -1)
                nc.scalar.activation(q_part(h), bank[:, 2 + h % 2, 0:256], ACT.Copy).then_inc(qT_pe, 1)

            def exp_scores(n, last):
                act.wait_ge(e_act, 1)
                act.sem_inc(e_act, -1)
                of_pairs = gates[:, n * PAIR:(last + 1) * PAIR]
                nc.scalar.activation(of_pairs, of_pairs, ACT.Exp).then_inc(e_dve, 1)

            def step(f, layer_f, first, more):
                choices(0, 3)
                keep_x()
                choices(3, 4)
                query(4)
                choices(4, 8)
                query(5)
                choices(8, 11)
                if more:
                    square_x(f)
                choices(11, 13)
                query(6)
                choices(13, 16)
                if more:
                    normed()
                choices(16, 17)
                query(7)
                choices(17, 25)
                exp_scores(1, PAIRS - 1)
                choices(25, 26)
                if not more:
                    choices(26, CHOICES)
                    return
                if first:
                    choices(26, 27)
                    step_sizes(layer_f)
                    choices(27, 30)
                    sines()
                    choices(30, 36)
                else:
                    choices(26, 36)
                ssm_input()
                choices(36, 43)
                pool_input()
                choices(43, 80)
                gelu_y()
                choices(80, 85)
                glu_gate()
                choices(85, 97)
                square_mixed()
                choices(97, 103)
                h_turned()
                choices(103, 106)
                query(0)
                choices(106, 109)
                query(1)
                choices(109, 116)
                query(2)
                choices(116, 117)
                exp_scores(0, 0)
                choices(117, 121)
                query(3)
                choices(121, CHOICES)

            act.wait_ge(consts_act, 1)
            act.sem_inc(consts_act, -1)
            act.sem_inc(diag_free_act, DIAGS - 1)
            square_x(0)
            step_sizes(0)
            normed()
            sines()
            ssm_input()
            pool_input()
            gelu_y()
            glu_gate()
            square_mixed()
            h_turned()
            query(0)
            query(1)
            exp_scores(0, 0)
            query(2)
            query(3)
            for layer in range(DEPTH):
                s0 = layer * TILES
                with act.Fori(s0, s0 + TILES - 1) as s:
                    step(s + 1, layer, False, True)
                if layer + 1 < DEPTH:
                    step(s0 + TILES, layer + 1, True, True)
            step(None, None, False, False)

        @block.tensor
        def _(pe):
            def choices(a, b):
                for k in range(a, b):
                    if k == 0:
                        pe.wait_ge(acc_free_pe, 1)
                        pe.sem_inc(acc_free_pe, -1)
                    if k in DVE_SUMS:
                        continue
                    pe.wait_ge(diag_pe, 1)
                    pe.sem_inc(diag_pe, -1)
                    nc.tensor.matmul(acc[:, 0:512], diag[:, DIAG_OF[k], :], slots[SLOT_OF[k]][:, D:D + 512],
                                     start=k == 0, stop=k == CHOICES - 1, skip_group_check=True).then_inc(diag_free_act, 1)
                    nc.tensor.matmul(acc[:, 512:1024], diag[:, DIAG_OF[k], :], slots[SLOT_OF[k]][:, D + 512:2 * D],
                                     start=k == 0, stop=k == CHOICES - 1, skip_group_check=True).then_inc(slot_free_pool, 1)
                if b == CHOICES:
                    pe.drain().then_inc(acc_dve, 1)

            def turn_maps():
                pe.wait_ge(bd_pe, 1)
                pe.sem_inc(bd_pe, -1)
                for ri in range(2):
                    for q in range(CT):
                        last = nc.tensor.transpose(bank[:, ri, q * P:(q + 1) * P],
                                                   h_next[:, ri * 512 + q * P:ri * 512 + (q + 1) * P], ident[:, :])
                last.then_inc(bdT_dve, 1)

            def turn_x():
                pe.wait_ge(xn_pe, 1)
                pe.sem_inc(xn_pe, -1)
                for k in range(KD):
                    last = nc.tensor.transpose(bank[:, k // 4, (k % 4) * P:(k % 4 + 1) * P],
                                               h_next[:, k * P:(k + 1) * P], ident[:, :])
                last.then_inc(hTp_dve, 1)

            def project(f, m):
                if m == 0:
                    pe.wait_ge(hT_pe, 1)
                    pe.sem_inc(hT_pe, -1)
                turns = (KD - m % WIN_SLOTS + WIN_SLOTS - 1) // WIN_SLOTS
                pe.wait_ge(win_in[m % WIN_SLOTS], (f * turns + m // WIN_SLOTS + 1) * 16)
                for k in range(KD):
                    last = nc.tensor.matmul(bank[:, 2 + m // CT, (m % CT) * P:(m % CT + 1) * P],
                                            win_sb[m % WIN_SLOTS][:, k, :], hT[:, k, :], start=k == 0, stop=k == KD - 1)
                    if k == 0 and m == CT:
                        last.then_inc(projA_act, 1)
                if m < KD - WIN_SLOTS:
                    last.then_inc(win_used_sp, 1)
                if m == KD - 1:
                    last.then_inc(projB_act, 1)

            def state_inputs(q, first=False):
                if q == 0:
                    if first:
                        pe.wait_ge(maps_pe, 1)
                        pe.sem_inc(maps_pe, -1)
                    pe.wait_ge(uT_pe, 1)
                    pe.sem_inc(uT_pe, -1)
                    pe.wait_ge(poolT_pe, 1)
                    pe.sem_inc(poolT_pe, -1)
                else:
                    pe.wait_ge(bu_free_pe, 1)
                    pe.sem_inc(bu_free_pe, -1)
                for i in range(4):
                    for ri in range(2):
                        last = nc.tensor.matmul(bank[:, i, ri * P:(ri + 1) * P], bT[ri][32 * i:32 * i + 32, q, :],
                                                uT[32 * i:32 * i + 32, q, :], start=True, stop=True)
                last.then_inc(bu_dve, 1)

            def state_outputs(q):
                pe.wait_ge(s_pe, 1)
                pe.sem_inc(s_pe, -1)
                a = (q % 2) * D
                for i in range(4):
                    for ri in range(2):
                        last = nc.tensor.matmul(ff[32 * i:32 * i + 32, 0, q * P:(q + 1) * P], cw[ri][:, 4 * q + i, :],
                                                work[:, a + ri * 512 + i * P:a + ri * 512 + (i + 1) * P],
                                                start=ri == 0, stop=ri == 1)
                if q == 3:
                    last.then_inc(y_dve, 1)
                else:
                    last.then_inc(s_used_dve, 1)

            def glu(n):
                if n == 0:
                    pe.wait_ge(y1_pe, 1)
                    pe.sem_inc(y1_pe, -1)
                for k in range(CT):
                    last = nc.tensor.matmul(ff[:, 1, n * P:(n + 1) * P], wglu_sb[:, k, n * P:(n + 1) * P], uT[:, k, :],
                                            start=k == 0, stop=k == CT - 1)
                if n == CT - 1:
                    last.then_inc(glu_act, 1)

            def mix_pools(layer, first, bank_n=1):
                pe.wait_ge(pooled_pe, 1)
                pe.sem_inc(pooled_pe, -1)
                if first:
                    pe.wait_ge(weights_in, 16 * 4 * (layer + 1))
                for g in range(CT):
                    last = nc.tensor.matmul(ff[:, bank_n, g * P:(g + 1) * P], wpool_sb[:, g, :], hT[:, CT + g, :],
                                            start=True, stop=True)
                last.then_inc(poolmix_dve, 1)

            def project_out(half, i, layer, first):
                n, k = i // CT, i % CT
                if half == 1 and i == 0:
                    pe.wait_ge(mixB_pe, 1)
                    pe.sem_inc(mixB_pe, -1)
                    pe.wait_ge(bu_free_pe, 1)
                    pe.sem_inc(bu_free_pe, -1)
                    if first:
                        pe.wait_ge(wout_in, 16 * (layer + 1))
                dst = bank[:, 2 + n, :] if half == 1 else ff[:, n, :]
                last = nc.tensor.matmul(dst, hT[:, half * CT + k, :], wout_sb[:, half * CT + k, n * 512:(n + 1) * 512],
                                        start=k == 0, stop=k == CT - 1, skip_group_check=True)
                if half == 0 and i == 2 * CT - 1:
                    last.then_inc(outA_dve, 1)

            def sums():
                pe.wait_ge(mixA_pe, 1)
                pe.sem_inc(mixA_pe, -1)
                for half, squares in ((0, work[:, 512:1024]), (1, h_next[:, 512:1024])):
                    for k in range(CT):
                        last = nc.tensor.matmul(bank[:, 1, half:half + 1], squares[:, k * P:(k + 1) * P], ones[:, :],
                                                start=k == 0, stop=k == CT - 1)
                last.then_inc(sums_dve, 1)

            def turn_h():
                pe.wait_ge(h_pe, 1)
                pe.sem_inc(h_pe, -1)
                for k in range(KD):
                    last = nc.tensor.transpose(bank[:, k // 4, (k % 4) * P:(k % 4 + 1) * P],
                                               h_next[:, k * P:(k + 1) * P], ident[:, :])
                last.then_inc(hT2_act, 1)

            def query(h, half):
                for k in range(KD):
                    last = nc.tensor.matmul(bank[:, 2 + h % 2, half * P:(half + 1) * P],
                                            wq_sb[:, k, (2 * h + half) * P:(2 * h + half + 1) * P], hT[:, k, :],
                                            start=k == 0, stop=k == KD - 1)
                if half == 1:
                    last.then_inc(q_act, 1)

            def scores(h, begin=False):
                pe.wait_ge(qT_pe, 1)
                pe.sem_inc(qT_pe, -1)
                if not begin:
                    pe.wait_ge(score_free_pe, 1)
                    pe.sem_inc(score_free_pe, -1)
                for half in range(2):
                    last = nc.tensor.matmul(ff[:, h % 2, half * P:(half + 1) * P], q_part(h)[:, half * P:(half + 1) * P],
                                            keys_sb[:, half, :],
                                            start=True, stop=True)
                last.then_inc(score_dve, 1)

            def step(f, layer_f, first, more):
                at = 0
                for h, c in zip(range(4, HEADS), (0, 4, 9, 13)):
                    choices(at, c)
                    if h > 4:
                        scores(h - 1)
                    query(h, 0)
                    choices(c, c + 2)
                    query(h, 1)
                    at = c + 2
                choices(at, 17)
                if more:
                    turn_x()
                scores(HEADS - 1)
                choices(17, 20)
                if not more:
                    choices(20, CHOICES)
                    return
                at = 20
                for m, c in enumerate((23, 25, 30, 32, 34, 37, 39, 41)):
                    choices(at, c)
                    project(f, m)
                    at = c
                    if first and m == 3:
                        turn_maps()
                choices(at, 44)
                state_inputs(0, first)
                at = 44
                for q in range(1, 4):
                    choices(at, 42 + 8 * q)
                    state_inputs(q)
                    choices(42 + 8 * q, 47 + 8 * q)
                    state_outputs(q - 1)
                    at = 47 + 8 * q
                    if q == 2:
                        mix_pools(layer_f, first)
                choices(at, 72)
                for i in range(2 * CT):
                    project_out(1, i, layer_f, first)
                    choices(72 + i, 73 + i)
                    if i == CT:
                        state_outputs(3)
                choices(72 + 2 * CT, 81)
                for n in range(CT):
                    glu(n)
                    choices(81 + n, 82 + n)
                choices(85, 86)
                sums()
                for i in range(2 * CT):
                    project_out(0, i, layer_f, first)
                    choices(86 + i, 87 + i)
                choices(86 + 2 * CT, 102)
                turn_h()
                choices(102, 103)
                if first:
                    pe.wait_ge(wq_in, 16 * (layer_f + 1))
                pe.wait_ge(hT2_pe, 1)
                pe.sem_inc(hT2_pe, -1)
                query(0, 0)
                choices(103, 105)
                query(0, 1)
                choices(105, 107)
                query(1, 0)
                scores(0)
                choices(107, 108)
                query(1, 1)
                choices(108, 111)
                scores(1)
                choices(111, 112)
                query(2, 0)
                choices(112, 114)
                query(2, 1)
                choices(114, 117)
                scores(2)
                query(3, 0)
                choices(117, 119)
                query(3, 1)
                choices(119, 122)
                scores(3)
                choices(122, CHOICES)

            pe.wait_ge(consts_pe, 1)
            pe.sem_inc(consts_pe, -1)
            pe.sem_inc(acc_free_pe, 1)
            turn_x()
            for m in range(KD):
                project(0, m)
                if m == 5:
                    turn_maps()
            state_inputs(0, True)
            for q in range(1, 4):
                state_inputs(q)
                state_outputs(q - 1)
            state_outputs(3)
            for n in range(CT):
                glu(n)
            mix_pools(0, True, 0)
            for i in range(2 * CT):
                project_out(1, i, 0, True)
            sums()
            for i in range(2 * CT):
                project_out(0, i, 0, True)
            turn_h()
            pe.wait_ge(hT2_pe, 1)
            pe.sem_inc(hT2_pe, -1)
            pe.wait_ge(wq_in, 16)
            for h in range(4):
                query(h, 0)
                query(h, 1)
                scores(h, begin=h < 2)
            for layer in range(DEPTH):
                s0 = layer * TILES
                with pe.Fori(s0, s0 + TILES - 1) as s:
                    step(s + 1, layer, False, True)
                if layer + 1 < DEPTH:
                    step(s0 + TILES, layer + 1, True, True)
            step(None, None, False, False)

        @block.vector
        def _(dve):
            V = nc.vector

            def tt(o, a, b, op):
                return V.tensor_tensor(o, a, b, op)

            def add_row(k):
                dve.wait_ge(scale_dve, 1)
                dve.sem_inc(scale_dve, -1)
                V.scalar_tensor_tensor(x_pend[:, :], slots[SLOT_OF[k]][:, D:2 * D], dots[:, k % DOTS:k % DOTS + 1],
                                       x_pend[:, :], ALU.mult, ALU.add).then_inc(dve_own, 1)
                dve.wait_ge(dve_own, 1)
                dve.sem_inc(dve_own, -1)
                dve.sem_inc(slot_free_by_dve_pool, 1)

            def choices(s, a, b):
                for k in range(a, b):
                    j = SLOT_OF[k]
                    dve.wait_ge(row_in[j], (s * TURNS[j] + TURN[k] + 1) * 16)
                    V.tensor_tensor_reduce(out=slots[j][:, 0:D], in0=slots[j][:, 0:D], in1=h_dot[:, :],
                                           scale=1.0, scalar=0.0, op0=ALU.mult, op1=ALU.add,
                                           accum_out=dots[:, k % DOTS:k % DOTS + 1]).then_inc(dot_act, 1)
                    if k - SUM_LAG in DVE_SUMS:
                        add_row(k - SUM_LAG)

            def mean_square(src, dst, n, width):
                V.tensor_scalar(stat[:, dst:dst + n], stat[:, src:src + n], 1.0 / width, EPS, ALU.mult,
                                ALU.add).then_inc(dve_own, 1)
                dve.wait_ge(dve_own, 1)
                dve.sem_inc(dve_own, -1)
                dve.sem_inc(ms_pool, 1)

            def add_experts():
                dve.wait_ge(acc_dve, 1)
                dve.sem_inc(acc_dve, -1)
                tt(x_pend[:, :], x_pend[:, :], acc[:, :], ALU.add).then_inc(dve_own, 1)
                dve.wait_ge(dve_own, 1)
                dve.sem_inc(dve_own, -1)
                dve.sem_inc(acc_free_pe, 1)

            def handover():
                V.tensor_copy(h_dot[:, :], h_next[:, :]).then_inc(dve_own, 1)
                dve.wait_ge(dve_own, 1)
                dve.sem_inc(dve_own, -1)

            dt, lr, th, r, sh, s1, c1, ar, ai, zr, zi, t = (small[:, i, :] for i in range(12))
            lam_re, lam_im = par[:, LAM_RE:LAM_RE + BLOCKS], par[:, LAM_IM:LAM_IM + BLOCKS]

            def angles(layer):
                dve.wait_ge(set_dve, 1)
                dve.sem_inc(set_dve, -1)
                dve.wait_ge(par_in, 16 * (layer + 1))
                tt(lr, lam_re, dt, ALU.mult)
                tt(th, lam_im, dt, ALU.mult).then_inc(dve_own, 1)
                dve.wait_ge(dve_own, 1)
                dve.sem_inc(dve_own, -1)
                V.tensor_scalar(t, th, 1.0 / (2 * math.pi), ROUND, ALU.mult, ALU.add).then_inc(dve_own, 1)
                dve.wait_ge(dve_own, 1)
                dve.sem_inc(dve_own, -1)
                V.tensor_scalar(t, t, ROUND, None, ALU.subtract).then_inc(dve_own, 1)
                dve.wait_ge(dve_own, 1)
                dve.sem_inc(dve_own, -1)
                for part in (TWO_PI_1, TWO_PI_2, TWO_PI_3):
                    V.scalar_tensor_tensor(th, t, -part, th, ALU.mult, ALU.add).then_inc(dve_own, 1)
                    dve.wait_ge(dve_own, 1)
                    dve.sem_inc(dve_own, -1)
                V.tensor_scalar(th, th, PI_BELOW, -PI_BELOW, ALU.min, ALU.max).then_inc(dve_own, 1)
                dve.wait_ge(dve_own, 1)
                dve.sem_inc(dve_own, -1)
                dve.sem_inc(set_act, 1)

            def input_scales():
                dve.wait_ge(set_dve, 1)
                dve.sem_inc(set_dve, -1)
                tt(c1, sh, sh, ALU.mult).then_inc(dve_own, 1)
                dve.wait_ge(dve_own, 1)
                dve.sem_inc(dve_own, -1)
                V.tensor_scalar(c1, c1, -2.0, 1.0, ALU.mult, ALU.add).then_inc(dve_own, 1)
                dve.wait_ge(dve_own, 1)
                dve.sem_inc(dve_own, -1)
                tt(ar, r, c1, ALU.mult)
                tt(ai, r, s1, ALU.mult).then_inc(dve_own, 1)
                dve.wait_ge(dve_own, 1)
                dve.sem_inc(dve_own, -1)
                tt(t, lam_re, lam_re, ALU.mult)
                tt(sh, lam_im, lam_im, ALU.mult).then_inc(dve_own, 1)
                dve.wait_ge(dve_own, 1)
                dve.sem_inc(dve_own, -1)
                tt(t, t, sh, ALU.add).then_inc(dve_own, 1)
                dve.wait_ge(dve_own, 1)
                dve.sem_inc(dve_own, -1)
                V.reciprocal(t, t)
                V.tensor_scalar(ar, ar, 1.0, None, ALU.subtract).then_inc(dve_own, 1)
                dve.wait_ge(dve_own, 1)
                dve.sem_inc(dve_own, -1)
                tt(zr, ar, lam_re, ALU.mult)
                tt(sh, ai, lam_im, ALU.mult).then_inc(dve_own, 1)
                dve.wait_ge(dve_own, 1)
                dve.sem_inc(dve_own, -1)
                tt(zr, zr, sh, ALU.add).then_inc(dve_own, 1)
                dve.wait_ge(dve_own, 1)
                dve.sem_inc(dve_own, -1)
                tt(zi, ai, lam_re, ALU.mult)
                tt(sh, ar, lam_im, ALU.mult).then_inc(dve_own, 1)
                dve.wait_ge(dve_own, 1)
                dve.sem_inc(dve_own, -1)
                tt(zi, zi, sh, ALU.subtract).then_inc(dve_own, 1)
                dve.wait_ge(dve_own, 1)
                dve.sem_inc(dve_own, -1)
                tt(zr, zr, t, ALU.mult)
                tt(zi, zi, t, ALU.mult).then_inc(dve_own, 1)
                dve.wait_ge(dve_own, 1)
                dve.sem_inc(dve_own, -1)

            def maps(layer):
                dve.wait_ge(bc_in, 16 * (layer + 1))
                raw = tab_c[:, :, :].rearrange("p a b -> p (a b)")
                b_re, b_im, c_re, c_im = (raw[:, i * BC:(i + 1) * BC].rearrange("p (b h) -> p b h", h=GROUP_CH)
                                          for i in range(4))
                bd = [h_next[:, i * 512:(i + 1) * 512].rearrange("p (b c) -> p b c", c=BLOCK_CH) for i in range(2)]
                flat = poolT[:, :, :].rearrange("p a b -> p (a b)")
                t1 = flat[:, 0:BC].rearrange("p (b h) -> p b h", h=GROUP_CH)
                t2 = flat[:, BC:2 * BC].rearrange("p (b h) -> p b h", h=GROUP_CH)
                zrb = zr.unsqueeze(2).broadcast_to([P, BLOCKS, GROUP_CH])
                zib = zi.unsqueeze(2).broadcast_to([P, BLOCKS, GROUP_CH])
                V.memset(h_next[:, :], 0.0)
                V.memset(cw[0][:, :, :], 0.0)
                V.memset(cw[1][:, :, :], 0.0)
                for out_i, (p, q, op) in enumerate(((b_re, b_im, ALU.subtract), (b_im, b_re, ALU.add))):
                    tt(t1, p, zrb, ALU.mult)
                    tt(t2, q, zib, ALU.mult).then_inc(dve_own, 1)
                    dve.wait_ge(dve_own, 1)
                    dve.sem_inc(dve_own, -1)
                    for half in range(2):
                        rows, cols = slice(64 * half, 64 * half + 64), slice(16 * half, 16 * half + 16)
                        tt(bd[out_i][rows, :, cols], t1[rows], t2[rows], op).then_inc(dve_own, 1)
                        dve.wait_ge(dve_own, 1)
                        dve.sem_inc(dve_own, -1)
                dve.sem_inc(bd_pe, 1)
                for half in range(2):
                    rows, cols = slice(64 * half, 64 * half + 64), slice(16 * half, 16 * half + 16)
                    V.tensor_copy(cw[0][rows, :, cols], c_re[rows])
                    V.tensor_scalar(cw[1][rows, :, cols], c_im[rows], -1.0, None, ALU.mult).then_inc(dve_own, 1)
                    dve.wait_ge(dve_own, 1)
                    dve.sem_inc(dve_own, -1)

            def keep_maps():
                dve.wait_ge(bdT_dve, 1)
                dve.sem_inc(bdT_dve, -1)
                for ri in range(2):
                    V.tensor_copy(bT[ri][:, :, :].rearrange("p a b -> p (a b)"), bank[:, ri, :])
                V.memset(state[:, :, :], 0.0).then_inc(dve_own, 1)
                dve.wait_ge(dve_own, 1)
                dve.sem_inc(dve_own, -1)
                dve.sem_inc(maps_pe, 1)

            def tables(first_n, last_n):
                if first_n == 1:
                    V.tensor_copy(tab_c[:, :, 0:1], c1.unsqueeze(2))
                    V.tensor_copy(tab_s[:, :, 0:1], s1.unsqueeze(2)).then_inc(dve_own, 1)
                    dve.wait_ge(dve_own, 1)
                    dve.sem_inc(dve_own, -1)
                n = first_n
                while n < last_n:
                    new = tab[:, :, :, n:2 * n]
                    turned = h_next[:, 0:2 * BLOCKS * n].rearrange("p (a b n) -> p a b n", a=2, n=n)
                    cn = tab_c[:, :, n - 1:n].unsqueeze(1).broadcast_to([P, 2, BLOCKS, n])
                    sn = tab_s[:, :, n - 1:n].unsqueeze(1).broadcast_to([P, 2, BLOCKS, n])
                    tt(new, tab[:, :, :, 0:n], cn, ALU.mult)
                    tt(turned, tab[:, :, :, 0:n], sn, ALU.mult).then_inc(dve_own, 1)
                    dve.wait_ge(dve_own, 1)
                    dve.sem_inc(dve_own, -1)
                    tt(new[:, 0], new[:, 0], turned[:, 1], ALU.subtract)
                    tt(new[:, 1], new[:, 1], turned[:, 0], ALU.add).then_inc(dve_own, 1)
                    dve.wait_ge(dve_own, 1)
                    dve.sem_inc(dve_own, -1)
                    n *= 2

            def square_x():
                dve.wait_ge(sq_dve, 1)
                dve.sem_inc(sq_dve, -1)
                mean_square(2, 0, 1, D)

            def halo(first):
                if first:
                    V.memset(poolT[:, :, 0:HALO], 0.0).then_inc(dve_own, 1)
                    dve.wait_ge(dve_own, 1)
                    dve.sem_inc(dve_own, -1)
                else:
                    V.tensor_copy(poolT[:, :, 0:HALO], poolT[:, :, P:P + HALO]).then_inc(dve_own, 1)
                    dve.wait_ge(dve_own, 1)
                    dve.sem_inc(dve_own, -1)
                dve.sem_inc(halo_act, 1)

            def turned_x(layer):
                dve.wait_ge(hTp_dve, 1)
                dve.sem_inc(hTp_dve, -1)
                dve.wait_ge(par_in, 16 * (layer + 1))
                gain = par[:, G_MIX:G_MIX + KD].unsqueeze(2).broadcast_to([P, KD, P])
                tt(hT[:, :, :], bank[:, 0:2, :].rearrange("p a (b c) -> p (a b) c", c=P), gain, ALU.mult).then_inc(hT_pe, 1)

            def tabs(q):
                return [t[:, 4 * q:4 * q + 4, :].unsqueeze(2).broadcast_to([P, 4, 2, HALF]) for t in (tab_c, tab_s)]

            def spaces(q):
                a = (q % 2) * D
                return piece(a, 4, 2, HALF), piece(2048, 4, 2, HALF), piece(a + 512, 4, 2, HALF), piece(2560, 4, 2, HALF)

            def scan(q, half):
                re, re_out, im, im_out = spaces(q)
                for i in range(4):
                    b = 4 * q + i
                    decay = small[:, 3, b:b + 1].broadcast_to([P, HALF])
                    V.tensor_tensor_scan(re_out[:, i, half, :], decay, re[:, i, half, :], state[:, 0, b:b + 1],
                                         ALU.mult, ALU.add)
                    last = V.tensor_tensor_scan(im_out[:, i, half, :], decay, im[:, i, half, :], state[:, 1, b:b + 1],
                                                ALU.mult, ALU.add)
                last.then_inc(dve_own, 1)
                dve.wait_ge(dve_own, 1)
                dve.sem_inc(dve_own, -1)

            def turn_back(q):
                if q == 0:
                    dve.wait_ge(uT_dve, 1)
                    dve.sem_inc(uT_dve, -1)
                dve.wait_ge(bu_dve, 1)
                dve.sem_inc(bu_dve, -1)
                if q >= 2:
                    dve.wait_ge(s_used_dve, 1)
                    dve.sem_inc(s_used_dve, -1)
                A, B, C, E = spaces(q)
                tc, ts = tabs(q)
                re = bank[:, :, 0:P].rearrange("p i (h t) -> p i h t", h=2)
                im = bank[:, :, P:2 * P].rearrange("p i (h t) -> p i h t", h=2)
                tt(A, re, tc, ALU.mult)
                tt(B, im, ts, ALU.mult)
                tt(C, im, tc, ALU.mult)
                tt(E, re, ts, ALU.mult).then_inc(dve_own, 1)
                dve.wait_ge(dve_own, 1)
                dve.sem_inc(dve_own, -1)
                dve.sem_inc(bu_free_pe, 1)

            def first_half(q):
                A, B, C, E = spaces(q)
                tt(A, A, B, ALU.add)
                tt(C, C, E, ALU.subtract).then_inc(dve_own, 1)
                dve.wait_ge(dve_own, 1)
                dve.sem_inc(dve_own, -1)
                scan(q, 0)
                c64, s64 = (t[:, 4 * q:4 * q + 4, HALF - 1] for t in (tab_c, tab_s))
                zr, zi = B[:, :, 0, HALF - 1], E[:, :, 0, HALF - 1]
                for n, (u, v) in enumerate(((zr, c64), (zi, s64), (zr, s64), (zi, c64))):
                    last = tt(hand[:, n, :], u, v, ALU.mult)
                last.then_inc(dve_own, 1)
                dve.wait_ge(dve_own, 1)
                dve.sem_inc(dve_own, -1)
                tt(state[:, 0, 4 * q:4 * q + 4], hand[:, 0, :], hand[:, 1, :], ALU.subtract)
                tt(state[:, 1, 4 * q:4 * q + 4], hand[:, 2, :], hand[:, 3, :], ALU.add).then_inc(dve_own, 1)
                dve.wait_ge(dve_own, 1)
                dve.sem_inc(dve_own, -1)

            def second_half(q):
                scan(q, 1)
                A, B, C, E = spaces(q)
                tc, ts = tabs(q)
                tt(A, tc, B, ALU.mult)
                tt(C, ts, E, ALU.mult).then_inc(dve_own, 1)
                dve.wait_ge(dve_own, 1)
                dve.sem_inc(dve_own, -1)

            def turn_forth(q):
                A, B, C, E = spaces(q)
                tc, ts = tabs(q)
                tt(A, A, C, ALU.subtract)
                tt(E, tc, E, ALU.mult)
                tt(B, ts, B, ALU.mult).then_inc(dve_own, 1)
                dve.wait_ge(dve_own, 1)
                dve.sem_inc(dve_own, -1)
                tt(C, E, B, ALU.add).then_inc(dve_own, 1)
                dve.wait_ge(dve_own, 1)
                dve.sem_inc(dve_own, -1)
                dve.sem_inc(s_pe, 1)
                V.tensor_copy(state[:, 0, 4 * q:4 * q + 4], A[:, :, 1, HALF - 1])
                V.tensor_copy(state[:, 1, 4 * q:4 * q + 4], C[:, :, 1, HALF - 1]).then_inc(dve_own, 1)
                dve.wait_ge(dve_own, 1)
                dve.sem_inc(dve_own, -1)

            def skip():
                tt(uT[:, :, :], uT[:, :, :], par[:, D_SKIP:D_SKIP + CT].unsqueeze(2).broadcast_to([P, CT, P]),
                   ALU.mult).then_inc(dve_own, 1)
                dve.wait_ge(dve_own, 1)
                dve.sem_inc(dve_own, -1)

            def ssm_output():
                dve.wait_ge(y_dve, 1)
                dve.sem_inc(y_dve, -1)
                tt(uT[:, :, :], uT[:, :, :], ff[:, 0, :].rearrange("p (a b) -> p a b", a=CT), ALU.add).then_inc(y_act, 1)

            def windows(n, first):
                if n == 0:
                    dve.wait_ge(poolT_dve, 1)
                    dve.sem_inc(poolT_dve, -1)
                sums = [poolT[:, :, :]] + [h_next[:, a:a + (CT - i) * L].rearrange("p (a b) -> p a b", b=L)
                                           for i, a in enumerate((0, CT * L, 0, CT * L))]
                w = WINDOWS[n]
                lag = w // 2
                prev = sums[n] if n == 0 else sums[n][:, 1:, :]
                tt(sums[n + 1][:, :, w - 1:], prev[:, :, w - 1:], prev[:, :, w - 1 - lag:L - lag],
                   ALU.add).then_inc(dve_own, 1)
                dve.wait_ge(dve_own, 1)
                dve.sem_inc(dve_own, -1)
                V.scalar_tensor_tensor(hT[:, CT + n, :], sums[n + 1][:, 0, HALO:], 1.0 / w, poolT[:, n, HALO:],
                                       ALU.mult, ALU.subtract).then_inc(dve_own, 1)
                dve.wait_ge(dve_own, 1)
                dve.sem_inc(dve_own, -1)
                if first:
                    early = h_next[:, D - HALO:D]
                    tt(early, sums[n + 1][:, 0, HALO:2 * HALO], invcnt[:, n, :], ALU.mult).then_inc(dve_own, 1)
                    dve.wait_ge(dve_own, 1)
                    dve.sem_inc(dve_own, -1)
                    tt(hT[:, CT + n, 0:HALO], early, poolT[:, n, HALO:2 * HALO], ALU.subtract).then_inc(dve_own, 1)
                    dve.wait_ge(dve_own, 1)
                    dve.sem_inc(dve_own, -1)
                if n == len(WINDOWS) - 1:
                    dve.sem_inc(pooled_pe, 1)

            def pool_output(bank_n=1):
                dve.wait_ge(poolmix_dve, 1)
                dve.sem_inc(poolmix_dve, -1)
                yp = h_next[:, 0:512].rearrange("p (a b) -> p a b", a=CT)
                tt(yp, ff[:, bank_n, :].rearrange("p (a b) -> p a b", a=CT),
                   par[:, P_SCALE:P_SCALE + CT].unsqueeze(2).broadcast_to([P, CT, P]), ALU.mult).then_inc(dve_own, 1)
                dve.wait_ge(dve_own, 1)
                dve.sem_inc(dve_own, -1)
                tt(h_next[:, 512:1024].rearrange("p (a b) -> p a b", a=CT), yp, yp, ALU.mult)
                tt(hT[:, CT:2 * CT, :], yp, par[:, G_POOL:G_POOL + CT].unsqueeze(2).broadcast_to([P, CT, P]),
                   ALU.mult).then_inc(mixB_pe, 1)

            def gated():
                dve.wait_ge(sg_dve, 1)
                dve.sem_inc(sg_dve, -1)
                tt(uT[:, :, :], uT[:, :, :], piece(0, CT, P), ALU.mult).then_inc(dve_own, 1)
                dve.wait_ge(dve_own, 1)
                dve.sem_inc(dve_own, -1)
                tt(piece(512, CT, P), uT[:, :, :], uT[:, :, :], ALU.mult)
                tt(hT[:, 0:CT, :], uT[:, :, :], par[:, G_SSM:G_SSM + CT].unsqueeze(2).broadcast_to([P, CT, P]),
                   ALU.mult).then_inc(mixA_pe, 1)

            def head_squares():
                dve.wait_ge(sums_dve, 1)
                dve.sem_inc(sums_dve, -1)
                V.tensor_scalar(stat[:, 4:6], bank[:, 1, 0:2], 1.0 / SSM, EPS, ALU.mult, ALU.add).then_inc(dve_own, 1)
                dve.wait_ge(dve_own, 1)
                dve.sem_inc(dve_own, -1)
                dve.sem_inc(ms_pool, 1)

            def residual():
                dve.wait_ge(rstd_dve, 1)
                dve.sem_inc(rstd_dve, -1)
                dve.wait_ge(outA_dve, 1)
                dve.sem_inc(outA_dve, -1)
                V.scalar_tensor_tensor(x_front[:, :], ff[:, :, :].rearrange("p a b -> p (a b)"), stat[:, 6:7],
                                       x_front[:, :], ALU.mult, ALU.add).then_inc(dve_own, 1)
                dve.wait_ge(dve_own, 1)
                dve.sem_inc(dve_own, -1)
                V.scalar_tensor_tensor(x_front[:, :], bank[:, 2:4, :].rearrange("p a b -> p (a b)"), stat[:, 7:8],
                                       x_front[:, :], ALU.mult, ALU.add).then_inc(dve_own, 1)
                dve.wait_ge(dve_own, 1)
                dve.sem_inc(dve_own, -1)
                dve.sem_inc(xmid_act, 1)
                dve.sem_inc(mix_done_sp, 1)

            def square_mixed(layer, first):
                if first:
                    dve.wait_ge(weights_in, 16 * 4 * (layer + 1))
                dve.wait_ge(sq_dve, 1)
                dve.sem_inc(sq_dve, -1)
                mean_square(10, 8, 1, D)

            def normed_mixed():
                dve.wait_ge(rstd_dve, 1)
                dve.sem_inc(rstd_dve, -1)
                V.scalar_tensor_tensor(h_next[:, :], x_front[:, :], stat[:, 9:10], gffn_sb[:, :], ALU.mult,
                                       ALU.mult).then_inc(dve_own, 1)
                dve.wait_ge(dve_own, 1)
                dve.sem_inc(dve_own, -1)
                dve.sem_inc(h_pe, 1)

            def top_keys(h):
                dve.wait_ge(score_dve, 1)
                dve.sem_inc(score_dve, -1)
                sc = [ff[:, h % 2, side * KEYS:(side + 1) * KEYS] for side in range(2)]
                rest = [piece(REST + side * KEYS, KEYS) for side in range(2)]
                V.max(v16[:, 0, 0:8], sc[0])
                V.max(v16[:, 1, 0:8], sc[1]).then_inc(dve_own, 1)
                dve.wait_ge(dve_own, 1)
                dve.sem_inc(dve_own, -1)
                V.match_replace(rest[0], v16[:, 0, 0:8], sc[0], LOWEST)
                V.match_replace(rest[1], v16[:, 1, 0:8], sc[1], LOWEST)
                V.max_index(i12[:, h, 0, 0:8], v16[:, 0, 0:8], sc[0])
                V.max_index(i12[:, h, 1, 0:8], v16[:, 1, 0:8], sc[1]).then_inc(dve_own, 1)
                dve.wait_ge(dve_own, 1)
                dve.sem_inc(dve_own, -1)
                dve.sem_inc(score_free_pe, 1)
                V.max(v16[:, 0, 8:16], rest[0])
                V.max(v16[:, 1, 8:16], rest[1]).then_inc(dve_own, 1)
                dve.wait_ge(dve_own, 1)
                dve.sem_inc(dve_own, -1)

            def top_pairs(h):
                rest = [piece(REST + side * KEYS, KEYS) for side in range(2)]
                V.max_index(i12[:, h, 0, 8:16], v16[:, 0, 8:16], rest[0])
                V.max_index(i12[:, h, 1, 8:16], v16[:, 1, 8:16], rest[1])
                cand, left = piece(CAND, TOPK * TOPK), piece(LEFT, TOPK * TOPK)
                tt(piece(CAND, TOPK, TOPK), v16[:, 0, :].unsqueeze(2).broadcast_to([P, TOPK, TOPK]),
                   v16[:, 1, :].unsqueeze(1).broadcast_to([P, TOPK, TOPK]), ALU.add).then_inc(dve_own, 1)
                dve.wait_ge(dve_own, 1)
                dve.sem_inc(dve_own, -1)
                V.max(best[:, h, 0:8], cand).then_inc(dve_own, 1)
                dve.wait_ge(dve_own, 1)
                dve.sem_inc(dve_own, -1)
                V.max_index(sel[:, h, 0:8], best[:, h, 0:8], cand)
                V.match_replace(left, best[:, h, 0:8], cand, LOWEST).then_inc(dve_own, 1)
                dve.wait_ge(dve_own, 1)
                dve.sem_inc(dve_own, -1)
                V.max(best[:, h, 8:16], left).then_inc(dve_own, 1)
                dve.wait_ge(dve_own, 1)
                dve.sem_inc(dve_own, -1)
                V.max_index(sel[:, h, 8:16], best[:, h, 8:16], left).then_inc(dve_own, 1)
                dve.wait_ge(dve_own, 1)
                dve.sem_inc(dve_own, -1)

            def lookup(n, side):
                digit = piece(MISC, PAIR).bitcast(U32)
                digit_f, ids = piece(MISC + 32, PAIR), piece(MISC + 64, 2, TOPK)
                row = piece(MISC + 96 + side * PAIR, PAIR)
                chosen = sel[:, 2 * n:2 * n + 2, :].rearrange("p h k -> p (h k)")
                if side == 0:
                    V.tensor_scalar(digit, chosen, 4, None, ALU.logical_shift_right)
                else:
                    V.tensor_scalar(digit, chosen, TOPK - 1, None, ALU.bitwise_and)
                V.tensor_copy(ids, i12[:, 2 * n:2 * n + 2, side, :]).then_inc(dve_own, 1)
                dve.wait_ge(dve_own, 1)
                dve.sem_inc(dve_own, -1)
                V.tensor_copy(digit_f, digit).then_inc(dve_own, 1)
                dve.wait_ge(dve_own, 1)
                dve.sem_inc(dve_own, -1)
                hot = piece(HOT, PAIR, TOPK)
                tt(hot, digit_f.unsqueeze(2).broadcast_to([P, PAIR, TOPK]),
                   iota16[:, :].unsqueeze(1).broadcast_to([P, PAIR, TOPK]), ALU.is_equal).then_inc(dve_own, 1)
                dve.wait_ge(dve_own, 1)
                dve.sem_inc(dve_own, -1)
                hot4 = piece(HOT, 2, TOPK * TOPK).rearrange("p h (k c) -> p h k c", k=TOPK)
                tt(hot4, hot4, ids.unsqueeze(2).broadcast_to([P, 2, TOPK, TOPK]), ALU.mult).then_inc(dve_own, 1)
                dve.wait_ge(dve_own, 1)
                dve.sem_inc(dve_own, -1)
                V.tensor_reduce(row, hot, AX_X, ALU.add).then_inc(dve_own, 1)
                dve.wait_ge(dve_own, 1)
                dve.sem_inc(dve_own, -1)

            def first_ids(n):
                lookup(n, 0)
                g3 = gates[:, n * PAIR:(n + 1) * PAIR].rearrange("p (h k) -> p h k", h=2)
                tt(g3, best[:, 2 * n:2 * n + 2, :], best[:, 2 * n:2 * n + 2, 0:1].broadcast_to([P, 2, TOPK]),
                   ALU.subtract).then_inc(dve_own, 1)
                dve.wait_ge(dve_own, 1)
                dve.sem_inc(dve_own, -1)
                if n in (0, PAIRS - 1):
                    dve.sem_inc(e_act, 1)

            def second_ids(n, layer):
                lookup(n, 1)
                row0, row1 = piece(MISC + 96, PAIR), piece(MISC + 96 + PAIR, PAIR)
                V.tensor_scalar(row0, row0, float(KEYS), float(layer * EXPERTS), ALU.mult, ALU.add).then_inc(dve_own, 1)
                dve.wait_ge(dve_own, 1)
                dve.sem_inc(dve_own, -1)
                tt(rows_of[:, n * PAIR:(n + 1) * PAIR], row0, row1, ALU.add).then_inc(dve_own, 1)
                dve.wait_ge(dve_own, 1)
                dve.sem_inc(dve_own, -1)
                dve.sem_inc(idx_pool, 1)

            def share_gates(n, last):
                dve.wait_ge(e_dve, 1)
                dve.sem_inc(e_dve, -1)
                heads = 2 * (last + 1 - n)
                g3 = gates[:, n * PAIR:(last + 1) * PAIR].rearrange("p (h k) -> p h k", h=heads)
                V.tensor_reduce(hsum[:, 0:heads], g3, AX_X, ALU.add).then_inc(dve_own, 1)
                dve.wait_ge(dve_own, 1)
                dve.sem_inc(dve_own, -1)
                V.reciprocal(hsum[:, 0:heads], hsum[:, 0:heads]).then_inc(dve_own, 1)
                dve.wait_ge(dve_own, 1)
                dve.sem_inc(dve_own, -1)
                tt(g3, g3, hsum[:, 0:heads].unsqueeze(2).broadcast_to([P, heads, TOPK]), ALU.mult).then_inc(dve_own, 1)
                dve.wait_ge(dve_own, 1)
                dve.sem_inc(dve_own, -1)
                dve.sem_inc(gates_act, last + 1 - n)

            def finished_tiles():
                dve.wait_ge(final_in, 16 * TILES)
                for t in range(TILES - 1):
                    V.tensor_tensor_reduce(out=final[4], in0=final[1 + t], in1=final[1 + t], scale=1.0, scalar=0.0,
                                           op0=ALU.mult, op1=ALU.add, accum_out=stat[:, 20 + t:21 + t]).then_inc(dve_own, 1)
                    dve.wait_ge(dve_own, 1)
                    dve.sem_inc(dve_own, -1)
                mean_square(20, 12, TILES - 1, D)

            def scale_finished():
                dve.wait_ge(rstd_dve, 1)
                dve.sem_inc(rstd_dve, -1)
                for t in range(TILES - 1):
                    V.scalar_tensor_tensor(final[1 + t], final[1 + t], stat[:, 15 + t:16 + t], final[0],
                                           ALU.mult, ALU.mult).then_inc(dve_own, 1)
                    dve.wait_ge(dve_own, 1)
                    dve.sem_inc(dve_own, -1)
                dve.sem_inc(final_sp, 1)

            def step(s, layer_s, f, layer_f, first, more):
                choices(s, 0, 2)
                first_ids(1)
                choices(s, 2, 4)
                second_ids(1, layer_s)
                choices(s, 4, 6)
                top_keys(4)
                choices(s, 6, 8)
                top_pairs(4)
                choices(s, 8, 11)
                top_keys(5)
                choices(s, 11, 13)
                if more:
                    square_x()
                top_pairs(5)
                choices(s, 13, 14)
                first_ids(2)
                choices(s, 14, 15)
                top_keys(6)
                choices(s, 15, 17)
                second_ids(2, layer_s)
                choices(s, 17, 18)
                top_pairs(6)
                choices(s, 18, 20)
                top_keys(7)
                choices(s, 20, 21)
                if more:
                    turned_x(layer_f)
                choices(s, 21, 22)
                top_pairs(7)
                choices(s, 22, 23)
                first_ids(3)
                choices(s, 23, 25)
                second_ids(3, layer_s)
                dve.sem_inc(front_done_sp, 1)
                choices(s, 25, 27)
                share_gates(1, PAIRS - 1)
                if not more:
                    choices(s, 27, 60)
                    finished_tiles()
                    choices(s, 60, 66)
                    scale_finished()
                    choices(s, 66, CHOICES)
                    return
                if first:
                    choices(s, 27, 28)
                    angles(layer_f)
                    choices(s, 28, 31)
                    input_scales()
                    choices(s, 31, 32)
                    maps(layer_f)
                    halo(True)
                    choices(s, 32, 37)
                    keep_maps()
                    choices(s, 37, 38)
                    tables(1, 8)
                    choices(s, 38, 40)
                    tables(8, 32)
                    choices(s, 40, 42)
                    tables(32, HALF)
                    choices(s, 42, 46)
                else:
                    halo(False)
                    choices(s, 27, 46)
                for q in range(4):
                    c = 46 + 8 * q
                    turn_back(q)
                    choices(s, c, c + 1)
                    if q < 2:
                        windows(2 * q, first)
                    choices(s, c + 1, c + 2)
                    first_half(q)
                    choices(s, c + 2, c + 4)
                    second_half(q)
                    choices(s, c + 4, c + 5)
                    if q < 2:
                        windows(2 * q + 1, first)
                    if q == 2:
                        pool_output()
                    choices(s, c + 5, c + 6)
                    turn_forth(q)
                    if q < 3:
                        choices(s, c + 6, c + 8)
                choices(s, 76, 77)
                skip()
                choices(s, 77, 79)
                ssm_output()
                choices(s, 79, 86)
                gated()
                choices(s, 86, 91)
                head_squares()
                choices(s, 91, 96)
                residual()
                choices(s, 96, 98)
                square_mixed(layer_f, first)
                choices(s, 98, 101)
                normed_mixed()
                choices(s, 101, 109)
                top_keys(0)
                choices(s, 109, 111)
                top_pairs(0)
                choices(s, 111, 113)
                top_keys(1)
                choices(s, 113, 115)
                top_pairs(1)
                choices(s, 115, 116)
                first_ids(0)
                choices(s, 116, 118)
                second_ids(0, layer_f)
                share_gates(0, 0)
                choices(s, 118, 120)
                top_keys(2)
                choices(s, 120, 122)
                top_pairs(2)
                choices(s, 122, 124)
                top_keys(3)
                choices(s, 124, 126)
                top_pairs(3)
                choices(s, 126, CHOICES)

            dve.wait_ge(consts_dve, 1)
            dve.sem_inc(consts_dve, -1)
            for n, w in enumerate(WINDOWS):
                V.tensor_scalar(invcnt[:, n, :], iota16[:, :], 1.0, float(w), ALU.add, ALU.min).then_inc(dve_own, 1)
                dve.wait_ge(dve_own, 1)
                dve.sem_inc(dve_own, -1)
            V.reciprocal(invcnt[:, :, :], invcnt[:, :, :]).then_inc(dve_own, 1)
            dve.wait_ge(dve_own, 1)
            dve.sem_inc(dve_own, -1)
            square_x()
            angles(0)
            turned_x(0)
            input_scales()
            maps(0)
            halo(True)
            keep_maps()
            tables(1, HALF)
            for q in range(4):
                turn_back(q)
                first_half(q)
                second_half(q)
                turn_forth(q)
            skip()
            ssm_output()
            for n in range(len(WINDOWS)):
                windows(n, True)
            pool_output(0)
            gated()
            head_squares()
            residual()
            square_mixed(0, True)
            normed_mixed()
            for h in range(2):
                top_keys(h)
                top_pairs(h)
            first_ids(0)
            second_ids(0, 0)
            share_gates(0, 0)
            for h in range(2, 4):
                top_keys(h)
                top_pairs(h)
            handover()
            for layer in range(DEPTH):
                s0 = layer * TILES
                with dve.Fori(s0, s0 + TILES - 1) as s:
                    step(s, layer, s + 1, layer, False, True)
                    add_experts()
                    dve.sem_inc(out_sp, 1)
                    handover()
                if layer + 1 < DEPTH:
                    step(s0 + TILES - 1, layer, s0 + TILES, layer + 1, True, True)
                    add_experts()
                    dve.sem_inc(out_sp, 1)
                    handover()
            step(STEPS - 1, DEPTH - 1, None, None, False, False)
            add_experts()
            V.tensor_tensor_reduce(out=h_dot[:, :], in0=x_pend[:, :], in1=x_pend[:, :], scale=1.0,
                                   scalar=0.0, op0=ALU.mult, op1=ALU.add, accum_out=stat[:, 23:24]).then_inc(dve_own, 1)
            dve.wait_ge(dve_own, 1)
            dve.sem_inc(dve_own, -1)
            mean_square(23, 18, 1, D)
            dve.wait_ge(rstd_dve, 1)
            dve.sem_inc(rstd_dve, -1)
            V.scalar_tensor_tensor(x_pend[:, :], x_pend[:, :], stat[:, 19:20], final[0], ALU.mult,
                                   ALU.mult).then_inc(dve_own, 1)
            dve.wait_ge(dve_own, 1)
            dve.sem_inc(dve_own, -1)
            dve.sem_inc(out_sp, 1)


def kernel(x, norm_mix, w_in, a_re, a_im, log_dt, b_re, b_im, c_re, c_im, d_skip, w_glu, b_glu, w_pool,
           pool_scale, g_out_ssm, g_out_pool, w_out, norm_ffn, w_q, k1, k2, u_experts, v_experts, norm_final):
    import numpy as np
    import concourse.bacc as bacc
    from concourse.bass_utils import run_bass_kernel_spmd as run

    (x, norm_mix, w_in, a_re, a_im, log_dt, b_re, b_im, c_re, c_im, d_skip, w_glu, b_glu, w_pool, pool_scale,
     g_out_ssm, g_out_pool, w_out, norm_ffn, w_q, k1, k2, u_experts, v_experts, norm_final) = (
        np.asarray(a) for a in (x, norm_mix, w_in, a_re, a_im, log_dt, b_re, b_im, c_re, c_im, d_skip, w_glu, b_glu,
                                w_pool, pool_scale, g_out_ssm, g_out_pool, w_out, norm_ffn, w_q, k1, k2, u_experts,
                                v_experts, norm_final))

    def rows(w, k):
        l, d, n = w.shape
        return w.reshape(l, k, d // k, n).transpose(0, 2, 1, 3)

    def states(a):
        return a.reshape(DEPTH, BLOCKS, P).transpose(0, 2, 1)

    def channels(a, k):
        return a.reshape(DEPTH, k, P).transpose(0, 2, 1)

    def maps(a):
        return a.reshape(DEPTH, BLOCKS, P, GROUP_CH).transpose(0, 2, 1, 3).reshape(DEPTH, P, BC)

    arrays = {
        "x": x.reshape(SEQ, D),
        "win": w_in.reshape(DEPTH, KD, P, KD, P).transpose(0, 3, 2, 1, 4),
        "wout": rows(w_out, KD),
        "wglu": rows(w_glu, CT),
        "wpool": w_pool.transpose(0, 2, 1, 3),
        "wq": rows(w_q, KD),
        "keys": np.stack([k1.transpose(0, 2, 1), k2.transpose(0, 2, 1)], axis=2),
        "params": np.concatenate([
            states(a_re), states(a_im), states(np.repeat(log_dt, STATE, axis=1)), channels(norm_mix, KD),
            channels(d_skip, CT), channels(b_glu, CT), channels(pool_scale, CT), channels(g_out_ssm, CT),
            channels(g_out_pool, CT)], axis=2),
        "bc": np.concatenate([maps(b_re), maps(b_im), maps(c_re.transpose(0, 1, 3, 2)),
                              maps(c_im.transpose(0, 1, 3, 2))], axis=2),
        "gffn": np.repeat(norm_ffn[:, None, :], P, axis=1),
        "gfinal": np.repeat(norm_final[None, :], P, axis=0),
        "uv": np.concatenate([u_experts, v_experts], axis=2).reshape(DEPTH * EXPERTS, 2 * D),
    }
    nc = bacc.Bacc("TRN2", target_bir_lowering=False, num_devices=1, dynamic_dma_scratch_size=4096)
    in_map, args = {}, []
    for name, a in arrays.items():
        a = np.ascontiguousarray(a)
        in_map[f"{name}_dram"] = a
        args.append(nc.dram_tensor(f"{name}_dram", a.shape, F32, kind="ExternalInput").ap())
    args.append(nc.dram_tensor("x_state_dram", (SEQ, D), F32, kind="Internal").ap())
    args.append(nc.dram_tensor("out_dram", (SEQ, D), F32, kind="ExternalOutput").ap())
    build(nc, *args)
    r = run(nc, [in_map], core_ids=[0])
    return r.results[0]["out_dram"].reshape(1, SEQ, D)
```
